# Optimizing a Trainium2 kernel written in Bass

```python
import math
import jax, jax.numpy as jnp
from jax import lax
import numpy as np

D_MODEL = 1024
BATCH = 1
SEQ = 1024
DEPTH = 1

CHUNK = 64
NORM_EPS = 1e-6
NEG_INF = -1e30
A_HEADS = 8
A_KV_HEADS = 2
A_HEAD_DIM = 64
A_GROUP = A_HEADS // A_KV_HEADS
A_WINDOW = 128
A_WINDOW_CHUNKS = A_WINDOW // CHUNK
A_WIDTH = A_HEADS * A_HEAD_DIM
B_HEADS = 8
B_Q_LORA = 384
B_KV_LORA = 256
B_NOPE = 64
B_ROPE = 32
B_V = 64
B_WIDTH = B_HEADS * B_V
ROPE_THETA = 10000.0
Q_BLOCK = 128
N_BRANCH = 2
IN_SIZES = [
    A_HEADS * A_HEAD_DIM,
    A_KV_HEADS * A_HEAD_DIM,
    A_KV_HEADS * A_HEAD_DIM,
    A_WIDTH,
    B_Q_LORA,
    B_KV_LORA,
    B_ROPE,
    B_WIDTH,
    N_BRANCH * D_MODEL,
]
IN_TOTAL = int(sum(IN_SIZES))
IN_SPLITS = [int(v) for v in np.cumsum(IN_SIZES)[:-1]]

kernel_name = "hybrid_swa_sink_mla_gated_block"

def rms_norm(x, g):
    xf = x.astype(jnp.float32)
    y = xf * lax.rsqrt(jnp.mean(xf * xf, axis=-1, keepdims=True) + NORM_EPS)
    return (y * g.astype(jnp.float32)).astype(x.dtype)

def alibi_slopes(n_heads):
    return jnp.asarray([2.0 ** (-8.0 * (h + 1) / n_heads) for h in range(n_heads)], dtype=jnp.float32)

def rope_tables(seq, dim):
    inv = 1.0 / (ROPE_THETA ** (jnp.arange(0, dim, 2, dtype=jnp.float32) / dim))
    ang = jnp.arange(seq, dtype=jnp.float32)[:, None] * inv[None, :]
    return jnp.cos(ang), jnp.sin(ang)

def apply_rope(x, cos, sin):
    xf = x.astype(jnp.float32)
    half = xf.shape[-1] // 2
    x1, x2 = xf[..., :half], xf[..., half:]
    return jnp.concatenate([x1 * cos - x2 * sin, x2 * cos + x1 * sin], axis=-1).astype(x.dtype)

def swa_sink_attention(q, k, v, sinks):
    bsz, seq = q.shape[0], q.shape[1]
    nc = seq // CHUNK
    wc = A_WINDOW_CHUNKS * CHUNK
    qc = q.reshape(bsz, nc, CHUNK, A_KV_HEADS, A_GROUP, A_HEAD_DIM)
    kc = k.reshape(bsz, nc, CHUNK, A_KV_HEADS, A_HEAD_DIM)
    vc = v.reshape(bsz, nc, CHUNK, A_KV_HEADS, A_HEAD_DIM)
    pad = ((0, 0), (A_WINDOW_CHUNKS - 1, 0), (0, 0), (0, 0), (0, 0))
    kp, vp = jnp.pad(kc, pad), jnp.pad(vc, pad)
    kw = jnp.concatenate([kp[:, w:w + nc] for w in range(A_WINDOW_CHUNKS)], axis=2)
    vw = jnp.concatenate([vp[:, w:w + nc] for w in range(A_WINDOW_CHUNKS)], axis=2)
    s = jnp.einsum('bnqkgd,bnskd->bnkgqs', qc, kw).astype(jnp.float32) * (A_HEAD_DIM ** -0.5)
    qi = jnp.arange(CHUNK)[:, None] + (A_WINDOW_CHUNKS - 1) * CHUNK
    kj = jnp.arange(wc)[None, :]
    dist = jnp.abs(qi - kj).astype(jnp.float32)
    bias = (-alibi_slopes(A_HEADS)[:, None, None] * dist[None]).reshape(A_KV_HEADS, A_GROUP, CHUNK, wc)
    s = s + bias[None, None]
    key_chunk = jnp.arange(nc)[:, None] - (A_WINDOW_CHUNKS - 1) + jnp.arange(wc)[None, :] // CHUNK
    valid = key_chunk >= 0
    s = jnp.where(valid[None, :, None, None, None, :], s, NEG_INF)
    sk = sinks.astype(jnp.float32).reshape(A_KV_HEADS, A_GROUP)[None, None, :, :, None, None]
    m = jnp.maximum(jnp.max(s, axis=-1, keepdims=True), sk)
    p = jnp.exp(s - m)
    probs = p / (jnp.sum(p, axis=-1, keepdims=True) + jnp.exp(sk - m))
    o = jnp.einsum('bnkgqs,bnskd->bnqkgd', probs.astype(v.dtype), vw)
    return o.reshape(bsz, seq, A_HEADS * A_HEAD_DIM)

def chunk_causal_block_attention(q, k, v):
    bsz, seq, nh, dqk = q.shape
    dv = v.shape[-1]
    nb = seq // Q_BLOCK
    qb = q.reshape(bsz, nb, Q_BLOCK, nh, dqk).transpose(1, 0, 2, 3, 4)
    key_pos = jnp.arange(seq)
    scale = dqk ** -0.5

    def one_block(args):
        qblk, start = args
        s = jnp.einsum('bqhd,bshd->bhqs', qblk, k).astype(jnp.float32) * scale
        qpos = start + jnp.arange(Q_BLOCK)
        limit = (qpos // CHUNK + 1) * CHUNK
        s = jnp.where(key_pos[None, :] < limit[:, None], s, NEG_INF)
        p = jax.nn.softmax(s, axis=-1)
        return jnp.einsum('bhqs,bshd->bqhd', p.astype(v.dtype), v)

    o = lax.map(one_block, (qb, jnp.arange(nb) * Q_BLOCK))
    return o.transpose(1, 0, 2, 3, 4).reshape(bsz, seq, nh * dv)

def setup_inputs(seed: int = 0) -> dict:
    key = jax.random.key(seed)
    ks = jax.random.split(key, 16)

    def w(k, shape, fan_in):
        return jax.random.normal(k, shape, jnp.float32) * (fan_in ** -0.5)

    def gain(k, shape):
        return 1.0 + 0.05 * jax.random.normal(k, shape, jnp.float32)

    return {
        "x": jax.random.normal(ks[0], (BATCH, SEQ, D_MODEL), jnp.float32),
        "pre_norm_g": gain(ks[1], (DEPTH, D_MODEL)),
        "w_in": w(ks[2], (DEPTH, D_MODEL, IN_TOTAL), D_MODEL),
        "a_sinks": 0.5 * jax.random.normal(ks[3], (DEPTH, A_HEADS), jnp.float32),
        "b_q_norm_g": gain(ks[4], (DEPTH, B_Q_LORA)),
        "b_w_uq": w(ks[5], (DEPTH, B_Q_LORA, B_HEADS * (B_NOPE + B_ROPE)), B_Q_LORA),
        "b_kv_norm_g": gain(ks[6], (DEPTH, B_KV_LORA)),
        "b_w_ukv": w(ks[7], (DEPTH, B_KV_LORA, B_HEADS * (B_NOPE + B_V)), B_KV_LORA),
        "a_w_o": w(ks[8], (DEPTH, A_WIDTH, D_MODEL), A_WIDTH),
        "b_w_o": w(ks[9], (DEPTH, B_WIDTH, D_MODEL), B_WIDTH),
        "w_out": w(ks[10], (DEPTH, D_MODEL, D_MODEL), D_MODEL),
        "post_norm_g": gain(ks[11], (DEPTH, D_MODEL)),
    }

def reference(x, pre_norm_g, w_in, a_sinks, b_q_norm_g, b_w_uq, b_kv_norm_g, b_w_ukv,
              a_w_o, b_w_o, w_out, post_norm_g):
    bsz, seq, _ = x.shape
    cos, sin = rope_tables(seq, B_ROPE)
    for l in range(DEPTH):
        h = rms_norm(x, pre_norm_g[l])
        proj = h @ w_in[l]
        qa, ka, va, ga, cq, ckv, kr, gb, gm = jnp.split(proj, IN_SPLITS, axis=-1)

        oa = swa_sink_attention(
            qa.reshape(bsz, seq, A_HEADS, A_HEAD_DIM),
            ka.reshape(bsz, seq, A_KV_HEADS, A_HEAD_DIM),
            va.reshape(bsz, seq, A_KV_HEADS, A_HEAD_DIM),
            a_sinks[l])
        ya = (oa * jax.nn.silu(ga)) @ a_w_o[l]

        qb = (rms_norm(cq, b_q_norm_g[l]) @ b_w_uq[l]).reshape(bsz, seq, B_HEADS, B_NOPE + B_ROPE)
        q_nope, q_rope = qb[..., :B_NOPE], qb[..., B_NOPE:]
        q_rope = apply_rope(q_rope, cos[:, None, :], sin[:, None, :])
        kvb = (rms_norm(ckv, b_kv_norm_g[l]) @ b_w_ukv[l]).reshape(bsz, seq, B_HEADS, B_NOPE + B_V)
        k_nope, vb = kvb[..., :B_NOPE], kvb[..., B_NOPE:]
        k_rope = apply_rope(kr, cos, sin)
        k_rope = jnp.broadcast_to(k_rope[:, :, None, :], (bsz, seq, B_HEADS, B_ROPE))
        ob = chunk_causal_block_attention(
            jnp.concatenate([q_nope, q_rope], axis=-1),
            jnp.concatenate([k_nope, k_rope], axis=-1),
            vb)
        yb = (ob * jax.nn.silu(gb)) @ b_w_o[l]

        g = jax.nn.sigmoid(gm.astype(jnp.float32)).astype(x.dtype).reshape(bsz, seq, N_BRANCH, D_MODEL)
        merged = g[:, :, 0, :] * ya + g[:, :, 1, :] * yb
        out = merged @ w_out[l]
        x = x + rms_norm(out, post_norm_g[l])
    return x


_drawn_inputs = setup_inputs


def setup_inputs(seed=0):
    import zlib

    import numpy as np

    out = dict(_drawn_inputs(seed))
    spreads = {}
    factors = {'b_q_norm_g': 3.929, 'a_sinks': 4.008}
    for name, (base, spread) in spreads.items():
        noise = np.random.default_rng([zlib.crc32(name.encode()), seed]).standard_normal(out[name].shape)
        drawn = base * np.exp(spread * noise) if base else spread * noise
        out[name] = __import__('jax').numpy.asarray(drawn.astype(out[name].dtype))
    for name, factor in factors.items():
        out[name] = (out[name] * factor).astype(out[name].dtype)
    return out
```

```python
import numpy as np
import concourse.bass as bass
from concourse import mybir
from contextlib import ExitStack

P = 128
SEQ, DM = 1024, 1024
CHUNK = 64
AH, AKV, AD = 8, 2, 64
AG = AH // AKV
BH, BN, BR, BV = 8, 64, 32, 64
BQK = BN + BR
QL, KL = 384, 256
W = 512
TT = SEQ // P
KD = DM // P
KQ, KK, KU = QL // P, KL // P, W // P
EPS = 1e-6
NEG = -1e30
THETA = 10000.0

C_QA = 0
C_KA = C_QA + AH * AD
C_VA = C_KA + AKV * AD
C_GA = C_VA + AKV * AD
C_CQ = C_GA + AH * AD
C_CKV = C_CQ + QL
C_KR = C_CKV + KL
C_GB = C_KR + BR
C_GM = C_GB + BH * BV
IN_TOTAL = C_GM + 2 * DM


def rope_table():
    inv = (1.0 / (np.float32(THETA) ** (np.arange(0, BR, 2, dtype=np.float32) / np.float32(BR)))).astype(np.float32)
    ang = (np.arange(SEQ, dtype=np.float32)[:, None] * inv[None, :]).astype(np.float32)
    cos, sin = np.cos(ang).astype(np.float32), np.sin(ang).astype(np.float32)
    return np.ascontiguousarray(np.stack([cos, sin]).reshape(2, TT, P, BR // 2).transpose(2, 0, 1, 3))


def alibi_table():
    q = np.arange(P)[:, None] + CHUNK
    k = np.arange(3 * CHUNK)[None, :]
    dist = np.abs(q - k).astype(np.float32)
    off = q // CHUNK - k // CHUNK
    seen = (off == 0) | (off == 1)
    slopes = [np.float32(2.0 ** (-8.0 * (h + 1) / AH)) for h in range(AH)]
    return np.ascontiguousarray(np.stack([np.where(seen, -s * dist, np.float32(NEG)) for s in slopes], 1).astype(np.float32))


def build(nc, x_d, pre_g_d, w_in_d, sinks_d, qg_d, w_uq_d, kvg_d, w_ukv_d, a_wo_d, b_wo_d,
          w_out_d, post_g_d, ident_d, rope_d, alibi_d, out_d):
    f32, f32r = mybir.dt.float32, mybir.dt.float32r
    ALU, ACT, AX = mybir.AluOpType, mybir.ActivationFunctionType, mybir.AxisListType
    KB = 1024
    BASE = 16512

    def at(name, shape, dt, kb):
        return nc.alloc_sbuf_tensor_at(name, shape, dt, offset=BASE + int(kb * KB))

    hT_h, hT_l = at("hT_h", [P, KD, SEQ], f32r, 0), at("hT_l", [P, KD, SEQ], f32r, 32)
    kT_h, kT_l = at("kT_h", [P, BH, SEQ], f32r, 0), at("kT_l", [P, BH, SEQ], f32r, 32)
    wv_h, wv_l = at("wv_h", [P, KK, W], f32r, 56), at("wv_l", [P, KK, W], f32r, 60)
    uT_h = [at("uaT_h", [P, KU, SEQ], f32r, 0), at("ubT_h", [P, KU, SEQ], f32r, 32)]
    uT_l = [at("uaT_l", [P, KU, SEQ], f32r, 16), at("ubT_l", [P, KU, SEQ], f32r, 48)]
    NMT = 3
    mT_h, mT_l = at("mT_h", [P, NMT, KD, P], f32r, 0), at("mT_l", [P, NMT, KD, P], f32r, 12)
    xres = at("xres", [P, 2, DM], f32, 24)
    NR = 8
    w_h, w_l = at("w_h", [P, NR, W], f32r, 64), at("w_l", [P, NR, W], f32r, 80)
    cqT_h, cqT_l = at("cqT_h", [P, KQ, SEQ], f32r, 64), at("cqT_l", [P, KQ, SEQ], f32r, 76)
    wk_h, wk_l = at("wk_h", [P, KK, W], f32r, 88), at("wk_l", [P, KK, W], f32r, 92)
    q_sb = at("q_sb", [P, 2, BH * BQK], f32, 88)
    onorm_b = at("onorm_b", [P, BH * BV], f32, 94)
    y_sb = at("y_sb", [P, 2, DM], f32, 64)
    pg = at("pg", [P, DM], f32, 80)
    junk_y = at("junk_y", [P, DM], f32, 84)
    NRAW = 4
    raw = at("raw", [P, NRAW, W], f32, 96)
    ga, gb = at("ga", [P, TT, W], f32, 104), at("gb", [P, TT, W], f32, 120)
    x_sb = [at(f"x_sb{t}", [P, DM], f32, (157 + 4 * t) if t < 4 else (104 + 4 * (t - 4))) for t in range(TT)]
    junk_x = at("junk_x", [P, DM], f32, 120)
    qaT_h, qaT_l = at("qaT_h", [P, AG, SEQ], f32r, 120), at("qaT_l", [P, AG, SEQ], f32r, 157)
    NPA = 3
    pT_a = at("pT_a", [P, NPA, W], f32, 136)
    alibi = at("alibi", [P, AH, 3 * CHUNK], f32, 142)
    onorm_a = at("onorm_a", [P, 4 * AD], f32, 148)
    cq = at("cq", [P, TT, QL], f32, 136)
    ckv = at("ckv", [P, TT, KL], f32, 149)
    NPB, NPT = 3, 4
    p_b = at("p_b", [P, NPB, SEQ], f32, 136)
    pT_b = at("pT_b", [P, NPT, W], f32, 148)
    v_b = at("v_b", [P, TT, BH * BV], f32, 157)
    merged = at("merged", [P, TT, DM], f32, 157)
    kz_h, kz_l = at("kz_h", [P, AKV, SEQ], f32r, 173), at("kz_l", [P, AKV, SEQ], f32r, 181)
    NST = 4
    stage = at("stage", [P, NST, W], f32, 173)
    kr = at("kr", [P, TT, BR], f32, 181)
    krr = at("krr", [P, TT, BR], f32, 182)
    kr2 = at("kr2", [P, TT, BR], f32, 183)
    junk_c = at("junk_c", [P, QL], f32, 184)
    ckvT_h, ckvT_l = at("ckvT_h", [P, KK, SEQ], f32r, 173), at("ckvT_l", [P, KK, SEQ], f32r, 181)
    qT_h, qT_l = at("qT_h", [P, 2, BH, P], f32r, 173), at("qT_l", [P, 2, BH, P], f32r, 181)
    va = at("va", [P, TT, AKV * AD], f32, 189)
    NSA = 3
    s_a = at("s_a", [P, NSA, 4, 2 * P], f32, 193)
    ka = at("ka", [P, TT, AKV * AD], f32, 193)
    small_a = at("small_a", [P, 4, 5, 4], f32, 205)
    wuq_h, wuq_l = at("wuq_h", [P, KQ, BH * BQK], f32r, 189), at("wuq_l", [P, KQ, BH * BQK], f32r, 198)
    NG = 3
    gate = at("gate", [P, NG, W], f32, 201)
    wo_at = [104 + 4 * j for j in range(13)] + [189 + 4 * j for j in range(3)]
    wo_h = [at(f"wo_h{j}", [P, W], f32r, kb) for j, kb in enumerate(wo_at)]
    wo_l = [at(f"wo_l{j}", [P, W], f32r, kb + 2) for j, kb in enumerate(wo_at)]
    ident = at("ident", [P, P], f32, 207)
    stats = at("stats", [P, 64], f32, 207.5)
    rope = at("rope", [P, 2, TT, BR // 2], f32, 186)
    rope_b = at("rope_b", [P, 2, TT, BR // 2], f32, 156)
    ss, rstd = stats[:, 0:8], stats[:, 8:16]
    g_pre, g_q, g_kv = stats[:, 16:24], stats[:, 24:27], stats[:, 27:29]
    sink, nsink = stats[:, 32:40], stats[:, 40:48]
    rs_b = stats[:, 48:64].rearrange("p (a h) -> p a h", a=2)
    negm_b = at("negm_b", [P, 4], f32, 207.75)
    rden_b = at("rden_b", [P, 8], f32, 207.78125)

    eps = at("eps", [P, 1], f32, 207.8125)

    gates_dram = nc.dram_tensor("gates_dram", (4 * TT, P, W), f32, kind="Internal").ap()

    ctx = ExitStack()
    with ctx:
        ps = ctx.enter_context(nc.psum_tensor("ps", [P, 8, W], f32))

        def sem(name):
            return ctx.enter_context(nc.semaphore(name))

        slices = []

        def add_slice(loads, n, g, hi, lo, slot=None):
            slices.append(dict(loads=loads, n=n, g=g, hi=hi, lo=lo, slot=slot))

        def rows(m, k):
            return m[k * P:(k + 1) * P, :]

        def ring_slice(loads, n, g):
            s = len(slices) % NR
            add_slice(loads, n, g, w_h[:, s, 0:n], w_l[:, s, 0:n], s)

        def in_slice(k, c0, n):
            ring_slice([((0, n), rows(w_in_d, k)[:, c0:c0 + n])], n, g_pre[:, k:k + 1])

        for k in range(KD):
            r = rows(w_in_d, k)
            ring_slice([((0, 256), r[:, C_KA:C_GA]), ((256, 512), r[:, C_CKV:C_KR])], W, g_pre[:, k:k + 1])
        for k in range(KD):
            r = rows(w_in_d, k)
            ring_slice([(("pair", g), r[:, C_QA + g * 256:C_QA + (g + 1) * 256].rearrange("p (j d) -> p j d", d=AD))
                        for g in range(AKV)], W, g_pre[:, k:k + 1])
        for k in range(KD):
            in_slice(k, C_GA, W)
        for k in range(KD):
            r = rows(w_in_d, k)
            ring_slice([((0, QL), r[:, C_CQ:C_CKV]), ((QL, QL + BR), r[:, C_KR:C_GB])], QL + BR, g_pre[:, k:k + 1])
        for k in range(KD):
            in_slice(k, C_GB, W)
        for b in range(4):
            for k in range(KD):
                in_slice(k, C_GM + b * W, W)
        S_UQ = len(slices)
        for k in range(KQ):
            for c in range(2):
                cs = slice(c * QL, (c + 1) * QL)
                add_slice([((0, QL), rows(w_uq_d, k)[:, cs])], QL, g_q[:, k:k + 1], wuq_h[:, k, cs], wuq_l[:, k, cs])
        S_UV = len(slices)
        for part, hi, lo in ((BN, wv_h, wv_l), (0, wk_h, wk_l)):
            for k in range(KK):
                src = rows(w_ukv_d, k).rearrange("p (h c) -> p h c", h=BH)[:, :, part:part + BN]
                add_slice([("heads", src)], W, g_kv[:, k:k + 1], hi[:, k, :], lo[:, k, :])
        S_AB = len(slices)
        for m, cb in ((a_wo_d, 0), (a_wo_d, 1), (b_wo_d, 0), (b_wo_d, 1)):
            for k in range(KU):
                s = (len(slices) - S_AB) % NR
                add_slice([((0, W), rows(m, k)[:, cb * W:(cb + 1) * W])], W, None, w_h[:, s, :], w_l[:, s, :], s)
        S_WO = len(slices)
        for j in range(2 * KD):
            k, cb = j // 2, j % 2
            add_slice([((0, W), rows(w_out_d, k)[:, cb * W:(cb + 1) * W])], W, None, wo_h[j][:, :], wo_l[j][:, :])
        NS = len(slices)
        raw_total = []
        filled = [0] * NRAW
        for n, s in enumerate(slices):
            filled[n % NRAW] += 16 * len(s["loads"])
            raw_total.append(filled[n % NRAW])

        raw_in = [sem(f"raw_in{r}") for r in range(NRAW)]
        hi_done, lo_done = sem("hi_done"), sem("lo_done")
        w_used = sem("w_used")
        consts_in = sem("consts_in")
        late_in = sem("late_in")
        x_in = [sem(f"x_in{t}") for t in range(TT)]
        x_sq, x_norm, x_T, hh_done, hl_done = (sem(n) for n in ("x_sq", "x_norm", "x_T", "hh_done", "hl_done"))
        blk_done = sem("blk_done")
        kvc_out = sem("kvc_out")
        ka_T, kz_hi, kz_lo, kz_zero = (sem(n) for n in ("ka_T", "kz_hi", "kz_lo", "kz_zero"))
        qa_hi, qa_lo = sem("qa_hi"), sem("qa_lo")
        ga_sig, ga_done, gb_sig, gb_done = (sem(n) for n in ("ga_sig", "ga_done", "gb_sig", "gb_done"))
        a_scores, a_added, a_nmax, a_exp, a_T, a_pT0, a_pT1, a_pv, a_out, s_zero = (
            sem("a_" + n) for n in ("scores", "added", "nmax", "exp", "T", "pT0", "pT1", "pv", "out", "szero"))
        cq_out, c_sq, c_norm, kr_roped = (sem(n) for n in ("cq_out", "c_sq", "c_norm", "kr_roped"))
        gm_out = sem("gm_out")
        gm_stored = [sem(f"gm_stored{i}") for i in range(NST)]
        k_done, k_hi = sem("k_done"), sem("k_hi")
        k_free = [sem(f"k_free{b}") for b in range(8)]
        mask_rows, kr_spread, qmask_rows = sem("mask_rows"), sem("kr_spread"), sem("qmask_rows")
        b_scores, b_nmax, b_exp, b_T, b_pT0, b_pT1, b_pv, b_out = (
            sem("b_" + n) for n in ("scores", "nmax", "exp", "T", "pT0", "pT1", "pv", "out"))
        b_free = [sem("b_free0"), sem("b_free1")]
        q_out, q_roped, qT_hi, qT_lo = (sem(n) for n in ("q_out", "q_roped", "qT_hi", "qT_lo"))
        u_T, u_hi, u_lo = sem("u_T"), sem("u_hi"), sem("u_lo")
        ab_done, ab_out, g_add = sem("ab_done"), sem("ab_out"), sem("g_add")
        gate_in = [sem(f"gate_in{i}") for i in range(NG)]
        m_T, m_hi, m_lo = sem("m_T"), sem("m_hi"), sem("m_lo")
        o_done, o_sq, o_y, o_add = sem("o_done"), sem("o_sq"), sem("o_y"), sem("o_add")
        xres_in = [sem("xres_in0"), sem("xres_in1")]
        stored = [sem("stored0"), sem("stored1")]
        eps_set = sem("eps_set")
        dve_step, act_step = sem("dve_step"), sem("act_step")

        NB0, NB = TT, 8 * 9
        A_UNITS = [(i, u) for i in range(TT) for u in range(2)]
        USES = [("Q", 0, 0), ("QT", 0, 0)]
        for i in range(TT):
            for h in range(BH):
                USES.append(("S", i, h))
                if i + 1 < TT and h == 2:
                    USES.append(("Q", i + 1, 0))
                if i + 1 < TT and h == 5:
                    USES.append(("QT", i + 1, 0))
        PIECES = {}
        SIDX = {}
        npiece = 0
        pt_evacs = [0, 0]
        for n, (kind, i, h) in enumerate(USES):
            if kind != "S":
                continue
            SIDX[(i, h)] = len(SIDX)
            PIECES[(i, h)] = []
            for t0 in range(0, i + 1, 4):
                PIECES[(i, h)].append((npiece, t0, min(i + 1, t0 + 4)))
                npiece += 1
        LAG_T, LAG_PV = 2, 3
        NU = len(USES)

        KUSES = [("kr", 0, 0), ("kr", 0, 1)] + [("ckv", k, hf) for hf in range(2) for k in range(KK)]
        KUSES += [("v", t, 0) for t in range(TT)] + [("cq", k, hf) for hf in range(2) for k in range(KQ)]
        KUSES += [("kn", pr, hf) for pr in range(BH // 2) for hf in range(2)]
        K_SPLIT = [u for u, k in enumerate(KUSES) if k[0] != "v"]
        KR_N, CKV_N = 2, 2 + 2 * KK
        V_END = CKV_N + TT

        block = ctx.enter_context(nc.Block())

        @block.sync
        def _(sp):
            sp.dma_start(x_sb[0][:, :], x_d[0:P, :]).then_inc(x_in[0], 16)
            for n, s in enumerate(slices):
                if n >= NRAW:
                    sp.wait_ge(lo_done, n - NRAW + 1)
                slot = raw[:, n % NRAW, :]
                for where, src in s["loads"]:
                    if where == "heads":
                        dst = slot.rearrange("p (h d) -> p h d", h=BH)
                    elif where[0] == "pair":
                        dst = slot.rearrange("p (j g d) -> p j g d", j=AG, g=AKV)[:, :, where[1], :]
                    else:
                        dst = slot[:, where[0]:where[1]]
                    sp.dma_start(dst, src).then_inc(raw_in[n % NRAW], 16)
            for t in range(TT):
                sp.wait_ge(o_add, t + 1)
                sp.dma_start(out_d[t * P:(t + 1) * P, :], y_sb[:, t % 2, :]).then_inc(stored[t % 2], 16)
            for r in range(2):
                sp.wait_ge(stored[r], 16 * (TT // 2))

        @block.gpsimd
        def _(pool):
            pool.dma_start(ident[:, :], ident_d).then_inc(consts_in, 16)
            pool.dma_start(g_pre, pre_g_d).then_inc(consts_in, 16)
            pool.dma_start(g_q, qg_d).then_inc(consts_in, 16)
            pool.dma_start(g_kv, kvg_d).then_inc(consts_in, 16)
            pool.dma_start(sink, sinks_d.partition_broadcast(P)).then_inc(late_in, 16)
            pool.dma_start(alibi[:, :, :], alibi_d).then_inc(late_in, 16)
            pool.memset(kz_h[64:128, 0, :].bitcast(f32), 0.0).then_inc(kz_zero, 1)
            pool.memset(kz_h[0:64, 1, :].bitcast(f32), 0.0).then_inc(kz_zero, 1)
            pool.memset(kz_l[64:128, 0, :].bitcast(f32), 0.0).then_inc(kz_zero, 1)
            pool.memset(kz_l[0:64, 1, :].bitcast(f32), 0.0).then_inc(kz_zero, 1)
            pool.wait_ge(ka_T, 2)
            for s in range(NSA):
                pool.memset(s_a[:, s, :, 0:CHUNK], 0.0).then_inc(s_zero, 1)
            pool.wait_ge(a_T, 2 * len(A_UNITS))
            pool.dma_start(rope[:, :, :, :], rope_d).then_inc(late_in, 16)
            for n in range(4 * TT):
                pool.wait_ge(gm_out, n + 1)
                pool.dma_start(gates_dram[n], stage[:, n % NST, :]).then_inc(gm_stored[n % NST], 16)
            pool.wait_ge(blk_done, NB)
            row = kT_h[BQK:BQK + 1, :, :].rearrange("p h s -> p (h s)").rearrange("p (b c) -> p b c", c=P).bitcast(f32)
            pool.memset(row[:, :, 0:CHUNK], 0.0).then_inc(mask_rows, 1)
            pool.memset(row[:, :, CHUNK:P], NEG).then_inc(mask_rows, 1)
            for b in range(KR_N):
                pool.wait_ge(k_free[b], 1)
            for c in range(2):
                cs = slice(c * W, (c + 1) * W)
                pool.tensor_copy(kT_h[BN:BQK, 1:BH, cs], kT_h[BN:BQK, 0:1, cs].bitcast(f32).to_broadcast([BR, BH - 1, W]))\
                    .then_inc(kr_spread, 1)
            pool.wait_ge(k_done, V_END)
            pool.dma_start(rope_b[:, :, :, :], rope_d).then_inc(late_in, 16)
            pool.memset(kT_l[BQK:BQK + 1, :, :].bitcast(f32), 0.0).then_inc(mask_rows, 1)
            for c in range(2):
                cs = slice(c * W, (c + 1) * W)
                pool.tensor_copy(kT_l[BN:BQK, 1:BH, cs], kT_l[BN:BQK, 0:1, cs].bitcast(f32).to_broadcast([BR, BH - 1, W]))\
                    .then_inc(kr_spread, 1)
            pool.wait_ge(k_done, len(KUSES))
            for a in range(2):
                pool.memset(qT_h[BQK:BQK + 1, a, :, 0:CHUNK].bitcast(f32), 1.0).then_inc(qmask_rows, 1)
                pool.memset(qT_h[BQK:BQK + 1, a, :, CHUNK:P].bitcast(f32), 0.0).then_inc(qmask_rows, 1)
                pool.memset(qT_l[BQK:BQK + 1, a, :, :].bitcast(f32), 0.0).then_inc(qmask_rows, 1)
            for i in range(NST):
                pool.wait_ge(gm_stored[i], 16 * (4 * TT // NST))
            pool.wait_ge(q_out, TT)
            for n in range(4 * TT + NG):
                if n >= NG and n - NG >= 2 * TT:
                    m = n - NG
                    cb, t = (m // TT) % 2, m % TT
                    pool.wait_ge(ab_out, m + 1)
                    dst = merged[:, t, cb * W:(cb + 1) * W]
                    pool.tensor_tensor(dst, dst, gate[:, m % NG, :], ALU.add).then_inc(g_add, 1)
                if n < 4 * TT:
                    if n >= NG:
                        pool.wait_ge(ab_out, n - NG + 1)
                    if n - NG >= 2 * TT:
                        pool.wait_ge(g_add, n - NG - 2 * TT + 1)
                    pool.dma_start(gate[:, n % NG, :], gates_dram[n]).then_inc(gate_in[n % NG], 16)
                if n in (2 * TT + 4, 2 * TT + 6):
                    r = (n - 2 * TT - 4) // 2
                    pool.dma_start(xres[:, r, :], x_d[r * P:(r + 1) * P, :]).then_inc(xres_in[r], 16)
            pool.wait_ge(ab_done, 4 * TT)
            pool.dma_start(pg[:, :], post_g_d.partition_broadcast(P)).then_inc(late_in, 16)
            for t in range(TT):
                pool.wait_ge(o_y, t + 1)
                pool.wait_ge(xres_in[t % 2], 16 * (t // 2 + 1))
                pool.tensor_tensor(y_sb[:, t % 2, :], y_sb[:, t % 2, :], xres[:, t % 2, :], ALU.add).then_inc(o_add, 1)
                if t + 2 < TT:
                    pool.wait_ge(o_add, t + 1)
                    pool.dma_start(xres[:, t % 2, :], x_d[(t + 2) * P:(t + 3) * P, :]).then_inc(xres_in[t % 2], 16)

        @block.scalar
        def _(act):
            def split_hi(n):
                s = slices[n]
                act.wait_ge(raw_in[n % NRAW], raw_total[n])
                if NR <= n < S_UQ:
                    blk, k = (n - NR) // KD, n % KD
                    if k == KD - 1:
                        act.wait_ge(blk_done, (blk + 1) * TT)
                    else:
                        act.wait_ge(w_used, blk * (KD - 1) + k + 1)
                if S_AB + NR <= n < S_WO:
                    act.wait_ge(ab_done, ((n - S_AB - NR) // KU + 1) * TT)
                src = raw[:, n % NRAW, 0:s["n"]]
                if s["g"] is None:
                    act.activation(s["hi"], src, ACT.Copy).then_inc(hi_done, 1)
                else:
                    act.activation(s["hi"], src, ACT.Copy, scale=s["g"]).then_inc(hi_done, 1)

            def bank_ready(n):
                act.wait_ge(blk_done, n + 1)

            for t in range(1, TT):
                act.dma_start(x_sb[t][:, :], x_d[t * P:(t + 1) * P, :]).then_inc(x_in[t], 16)

            steps = [0]

            def link(ins):
                steps[0] += 1
                ins.then_inc(act_step, 1)
                act.wait_ge(act_step, steps[0])

            def rms(col, width):
                return act.activation(col, col, ACT.Sqrt, bias=eps[:, :], scale=1.0 / width)

            def square_x(t):
                act.wait_ge(x_in[t], 16)
                link(act.activation(junk_x[:, :], x_sb[t][:, :], ACT.Square, accum_out=ss[:, t:t + 1]))
                rms(ss[:, t:t + 1], DM).then_inc(x_sq, 1)

            def hT_hi(t):
                for c in range(2):
                    act.wait_ge(x_T, 2 * t + c + 1)
                    act.activation(hT_h[:, 4 * c:4 * c + 4, t * P:(t + 1) * P],
                                   ps[:, (2 * t + c) % 4, :].rearrange("p (k s) -> p k s", k=4), ACT.Copy).then_inc(hh_done, 1)

            def kz_hi_out(half):
                act.wait_ge(ka_T, half + 1)
                act.wait_ge(kz_zero, 4)
                cs = slice(half * W, (half + 1) * W)
                for g in range(AKV):
                    rs = slice(64 * g, 64 * g + 64)
                    act.activation(kz_h[rs, g, cs], ps[rs, 7, :], ACT.Copy).then_inc(kz_hi, 1)

            def kvc(t):
                bank_ready(t)
                b = 4 + t % 3
                act.activation(ka[:, t, :], ps[:, b, 0:128], ACT.Copy)
                act.activation(va[:, t, :], ps[:, b, 128:256], ACT.Copy)
                act.activation(ckv[:, t, :], ps[:, b, 256:512], ACT.Copy).then_inc(kvc_out, 1)

            act.wait_ge(eps_set, 1)
            square_x(0)
            square_x(1)
            act.wait_ge(consts_in, 64)
            for n in range(4):
                split_hi(n)
            hT_hi(0)
            for n in range(4, 8):
                split_hi(n)
            for t in range(TT):
                if t + 2 < TT:
                    square_x(t + 2)
                if t + 1 < TT:
                    hT_hi(t + 1)
                if t == TT - 1:
                    for n in range(NR, 2 * NR - 1):
                        split_hi(n)
                kvc(t)
                if t == 4:
                    kz_hi_out(0)
            kz_hi_out(1)
            split_hi(2 * NR - 1)
            for n in range(2 * NR, 3 * NR - 1):
                split_hi(n)
            for b in range(8):
                bank_ready(NB0 + b)
                act.activation(qaT_h[:, b // 2, (b % 2) * W:(b % 2 + 1) * W], ps[:, b, :], ACT.Copy,
                               scale=AD ** -0.5).then_inc(qa_hi, 1)
            split_hi(3 * NR - 1)
            for n in range(3 * NR, 4 * NR - 1):
                split_hi(n)
            for t in range(TT):
                bank_ready(2 * TT + t)
                act.activation(ga[:, t, :], ps[:, t, :], ACT.Sigmoid).then_inc(ga_sig, 1)
            split_hi(4 * NR - 1)

            for n in range(len(A_UNITS) + LAG_T):
                if n < len(A_UNITS):
                    i, u = A_UNITS[n]
                    lo = P if i == 0 else CHUNK
                    act.wait_ge(a_nmax, n + 1)
                    for e in range(4):
                        act.activation(s_a[:, n % NSA, e, lo:], s_a[:, n % NSA, e, lo:], ACT.Exp,
                                       bias=small_a[:, n % 4, 0, e:e + 1], accum_out=small_a[:, n % 4, 1, e:e + 1])
                    act.activation(small_a[:, n % 4, 3, :], small_a[:, n % 4, 2, :], ACT.Exp).then_inc(a_exp, 1)
                if n >= LAG_T:
                    m = 2 * (n - LAG_T) + 1
                    act.wait_ge(a_T, m + 1)
                    if m >= NPA:
                        act.wait_ge(a_pv, m - NPA + 1)
                    if A_UNITS[n - LAG_T][0] == 0:
                        act.activation(pT_a[:, m % NPA, :].rearrange("p (e c s) -> p e c s", e=2, c=2)[:, :, 1, :],
                                       ps[:, 5, :].rearrange("p (e c s) -> p e c s", e=2, c=2)[:, :, 1, :], ACT.Copy).then_inc(a_pT1, 1)
                    else:
                        act.activation(pT_a[:, m % NPA, :], ps[:, 5, :], ACT.Copy).then_inc(a_pT1, 1)

            for n in range(4 * NR, 5 * NR - 1):
                split_hi(n)
            act.wait_ge(a_out, len(A_UNITS))
            for t in range(TT):
                bank_ready(3 * TT + t)
                act.activation(cq[:, t, :], ps[:, t, 0:QL], ACT.Copy)
                act.activation(kr[:, t, :], ps[:, t, QL:QL + BR], ACT.Copy).then_inc(cq_out, 1)
            split_hi(5 * NR - 1)
            act.wait_ge(cq_out, TT)
            for t in range(TT):
                link(act.activation(junk_c[:, :], cq[:, t, :], ACT.Square, accum_out=ss[:, t:t + 1]))
                link(act.activation(junk_c[:, 0:KL], ckv[:, t, :], ACT.Square, accum_out=rstd[:, t:t + 1]))
            rms(ss, QL).then_inc(c_sq, 1)
            rms(rstd, KL).then_inc(c_sq, 1)
            for n in range(5 * NR, 6 * NR - 1):
                split_hi(n)
            for t in range(TT):
                bank_ready(4 * TT + t)
                act.activation(gb[:, t, :], ps[:, t, :], ACT.Sigmoid).then_inc(gb_sig, 1)
            split_hi(6 * NR - 1)
            for b in range(4):
                ahead = list(range((6 + b) * NR, (7 + b) * NR)) if b < 3 else list(range(S_UQ, S_UV))
                for n in ahead[:NR - 1]:
                    split_hi(n)
                for t in range(TT):
                    n = b * TT + t
                    bank_ready((5 + b) * TT + t)
                    if n >= NST:
                        act.wait_ge(gm_stored[n % NST], 16 * (n // NST))
                    act.activation(stage[:, n % NST, :], ps[:, t, :], ACT.Sigmoid).then_inc(gm_out, 1)
                for n in ahead[NR - 1:]:
                    split_hi(n)
            act.wait_ge(blk_done, NB)
            for n in range(S_UV, S_AB):
                split_hi(n)

            for n, (kind, a, hf) in enumerate(KUSES):
                b = n % 8
                cs = slice(hf * W, (hf + 1) * W)
                act.wait_ge(k_done, n + 1)
                if n == 2:
                    for i in range(NST):
                        act.wait_ge(gm_stored[i], 16 * (4 * TT // NST))
                if kind == "kr":
                    act.activation(kT_h[BN:BQK, 0, cs], ps[0:BR, b, :], ACT.Copy).then_inc(k_hi, 1)
                elif kind == "ckv":
                    act.activation(ckvT_h[:, a, cs], ps[:, b, :], ACT.Copy).then_inc(k_hi, 1)
                elif kind == "cq":
                    act.activation(cqT_h[:, a, cs], ps[:, b, :], ACT.Copy).then_inc(k_hi, 1)
                elif kind == "kn":
                    act.activation(kT_h[0:BN, 2 * a, cs], ps[0:BN, b, :], ACT.Copy)
                    act.activation(kT_h[0:BN, 2 * a + 1, cs], ps[BN:2 * BN, b, :], ACT.Copy).then_inc(k_hi, 1)
                elif a % 2:
                    act.activation(v_b[:, a, :], ps[:, b, :], ACT.Copy).then_inc(k_free[b], 1)

            for n in range(NU + LAG_T):
                if n < NU:
                    kind, i, h = USES[n]
                    b0 = 2 * (n % 2)
                    if kind == "S":
                        m = SIDX[(i, h)]
                        keys = (i + 1) * P
                        act.wait_ge(b_nmax, m + 1)
                        if m >= NPB:
                            act.wait_ge(b_T, PIECES[(  (m - NPB) // BH, (m - NPB) % BH)][-1][0] + 1)
                        if h == 0 and i >= 2:
                            act.wait_ge(b_out, i - 1)
                        act.activation(p_b[:, m % NPB, 0:keys], ps[:, b0:b0 + 2, :].rearrange("p b c -> p (b c)")[:, 0:keys],
                                       ACT.Exp, bias=negm_b[:, m % 4:m % 4 + 1], accum_out=rs_b[:, i % 2, h:h + 1])\
                            .then_inc(b_exp, 1)
                        if i == TT - 1 and h < NR - 1:
                            split_hi(S_AB + h)
                    elif kind == "Q":
                        act.wait_ge(b_scores, n + 1)
                        if i == 0:
                            act.wait_ge(k_done, len(KUSES))
                        act.activation(q_sb[:, i % 2, :], ps[:, b0:b0 + 2, :].rearrange("p b c -> p (b c)")[:, 0:BH * BQK],
                                       ACT.Copy, scale=BQK ** -0.5).then_inc(q_out, 1)
                    else:
                        act.wait_ge(b_scores, n + 1)
                        act.activation(qT_h[0:BQK, i % 2, :, :], ps[0:BQK, b0:b0 + 2, :].rearrange("p b (h s) -> p (b h) s", h=4),
                                       ACT.Copy).then_inc(qT_hi, 1)
                if n >= LAG_T and USES[n - LAG_T][0] == "S":
                    for m, t0, t1 in PIECES[USES[n - LAG_T][1:]]:
                        if m % 2:
                            act.wait_ge(b_T, m + 1)
                            if m >= NPT:
                                act.wait_ge(b_pv, m - NPT + 1)
                            act.activation(pT_b[:, m % NPT, 0:(t1 - t0) * P], ps[:, 5, 0:(t1 - t0) * P], ACT.Copy)\
                                .then_inc(b_pT1, 1)

            def u_hi_out(m):
                br, t = m // TT, m % TT
                act.wait_ge(u_T, m + 1)
                act.activation(uT_h[br][:, :, t * P:(t + 1) * P], ps[:, 6 + m % 2, :].rearrange("p (k s) -> p k s", k=KU),
                               ACT.Copy).then_inc(u_hi, 1)

            def m_hi_out(t):
                for c in range(2):
                    act.wait_ge(m_T, 2 * t + c + 1)
                    if t >= NMT:
                        act.wait_ge(o_done, t - NMT + 1)
                    act.activation(mT_h[:, t % NMT, 4 * c:4 * c + 4, :].rearrange("p k s -> p (k s)"), ps[:, 6 + c, :],
                                   ACT.Copy).then_inc(m_hi, 1)

            u_hi_out(0)
            u_hi_out(1)
            for n in range(4 * TT):
                if n + 2 < 2 * TT:
                    u_hi_out(n + 2)
                if n == 1:
                    act.wait_ge(b_out, TT)
                    split_hi(S_AB + NR - 1)
                if n == TT:
                    for j in range(KU):
                        split_hi(S_AB + 2 * KU + j)
                if n == 2 * TT:
                    for j in range(KU):
                        split_hi(S_AB + 3 * KU + j)
                if n >= 2 * TT:
                    split_hi(S_WO + n - 2 * TT)
            m_hi_out(0)
            m_hi_out(1)
            for t in range(TT):
                if t + 2 < TT:
                    m_hi_out(t + 2)
                act.wait_ge(o_done, t + 1)
                if t >= 2:
                    act.wait_ge(o_y, t - 1)
                b0 = 2 * (t % 3)
                link(act.activation(junk_y[:, :], ps[:, b0:b0 + 2, :].rearrange("p b c -> p (b c)"), ACT.Square,
                                    accum_out=ss[:, t:t + 1]))
                rms(ss[:, t:t + 1], DM).then_inc(o_sq, 1)

        @block.vector
        def _(dve):
            steps = [0]

            def link(ins):
                steps[0] += 1
                ins.then_inc(dve_step, 1)
                dve.wait_ge(dve_step, steps[0])

            def invert(col):
                link(dve.reciprocal(col, col))

            def split_lo(n):
                s = slices[n]
                dve.wait_ge(hi_done, n + 1)
                src, hi = raw[:, n % NRAW, 0:s["n"]], s["hi"].bitcast(f32)
                if s["g"] is None:
                    dve.tensor_tensor(s["lo"], src, hi, ALU.subtract).then_inc(lo_done, 1)
                else:
                    dve.scalar_tensor_tensor(s["lo"], src, s["g"], hi, ALU.mult, ALU.subtract).then_inc(lo_done, 1)

            def norm_x(t):
                dve.wait_ge(x_sq, t + 1)
                invert(ss[:, t:t + 1])
                dve.tensor_scalar(x_sb[t][:, :], x_sb[t][:, :], ss[:, t:t + 1], None, ALU.mult).then_inc(x_norm, 1)

            def hT_lo(t):
                for c in range(2):
                    dve.wait_ge(hh_done, 2 * t + c + 1)
                    ks, cs = slice(4 * c, 4 * c + 4), slice(t * P, (t + 1) * P)
                    dve.tensor_tensor(hT_l[:, ks, cs], ps[:, (2 * t + c) % 4, :].rearrange("p (k s) -> p k s", k=4),
                                      hT_h[:, ks, cs].bitcast(f32), ALU.subtract).then_inc(hl_done, 1)

            def kz_lo_out(half):
                dve.wait_ge(kz_hi, 2 * half + 2)
                cs = slice(half * W, (half + 1) * W)
                for g in range(AKV):
                    rs = slice(64 * g, 64 * g + 64)
                    dve.tensor_tensor(kz_l[rs, g, cs], ps[rs, 7, :], kz_h[rs, g, cs].bitcast(f32), ALU.subtract)\
                        .then_inc(kz_lo, 1)

            dve.memset(eps[:, :], EPS).then_inc(eps_set, 1)
            norm_x(0)
            norm_x(1)
            for n in range(4):
                split_lo(n)
            hT_lo(0)
            for n in range(4, 8):
                split_lo(n)
            for t in range(TT):
                if t + 2 < TT:
                    norm_x(t + 2)
                if t + 1 < TT:
                    hT_lo(t + 1)
                if t == 4:
                    kz_lo_out(0)
            for n in range(NR, 2 * NR - 1):
                split_lo(n)
            kz_lo_out(1)
            for n in range(2 * NR - 1, 3 * NR - 1):
                split_lo(n)
            for b in range(8):
                dve.wait_ge(qa_hi, b + 1)
                cs = slice((b % 2) * W, (b % 2 + 1) * W)
                dve.scalar_tensor_tensor(qaT_l[:, b // 2, cs], ps[:, b, :], AD ** -0.5,
                                         qaT_h[:, b // 2, cs].bitcast(f32), ALU.mult, ALU.subtract).then_inc(qa_lo, 1)
            for n in range(3 * NR - 1, 4 * NR - 1):
                split_lo(n)
            for t in range(TT):
                dve.wait_ge(ga_sig, t + 1)
                dve.tensor_tensor(ga[:, t, :], ps[:, t, :], ga[:, t, :], ALU.mult).then_inc(ga_done, 1)
            split_lo(4 * NR - 1)

            dve.wait_ge(late_in, 32)
            link(dve.tensor_scalar(nsink, sink, -1.0, None, ALU.mult))
            dve.wait_ge(s_zero, NSA)
            heads2 = lambda v, u: v.rearrange("p (g c j) -> p c g j", g=AKV, c=2)[:, u]
            for n in range(len(A_UNITS) + LAG_PV):
                if n < len(A_UNITS):
                    i, u = A_UNITS[n]
                    lo = P if i == 0 else CHUNK
                    width = 2 * P - lo
                    b0 = 2 * (n % 2)
                    negm, esink = small_a[:, n % 4, 0, :], small_a[:, n % 4, 2, :]
                    dve.wait_ge(a_scores, n + 1)
                    if n >= NSA:
                        dve.wait_ge(a_T, 2 * (n - NSA) + 2)
                    for g in range(AKV):
                        h0 = g * AG + 2 * u
                        ins = dve.tensor_tensor(s_a[:, n % NSA, 2 * g:2 * g + 2, lo:],
                                                ps[:, b0 + g, :].rearrange("p (e c) -> p e c", e=2)[:, :, 0:width],
                                                alibi[:, h0:h0 + 2, 3 * CHUNK - width:], ALU.add)
                        ins.then_inc(a_added, 1)
                    dve.wait_ge(a_added, 2 * n + 2)
                    link(dve.tensor_reduce(negm, s_a[:, n % NSA, :, lo:], AX.X, ALU.max, negate=True))
                    n4 = negm.rearrange("p (g j) -> p g j", g=AKV)
                    link(dve.tensor_tensor(n4, n4, heads2(nsink, u), ALU.min))
                    dve.tensor_tensor(esink.rearrange("p (g j) -> p g j", g=AKV), n4, heads2(sink, u), ALU.add)\
                        .then_inc(a_nmax, 1)
                if LAG_T <= n < len(A_UNITS) + LAG_T:
                    m = 2 * (n - LAG_T)
                    dve.wait_ge(a_T, m + 1)
                    if m >= NPA:
                        dve.wait_ge(a_pv, m - NPA + 1)
                    if A_UNITS[n - LAG_T][0] == 0:
                        dve.tensor_copy(pT_a[:, m % NPA, :].rearrange("p (e c s) -> p e c s", e=2, c=2)[:, :, 1, :],
                                        ps[:, 4, :].rearrange("p (e c s) -> p e c s", e=2, c=2)[:, :, 1, :]).then_inc(a_pT0, 1)
                    else:
                        dve.tensor_copy(pT_a[:, m % NPA, :], ps[:, 4, :]).then_inc(a_pT0, 1)
                if n >= LAG_PV:
                    k = n - LAG_PV
                    i, u = A_UNITS[k]
                    den = small_a[:, k % 4, 4, :]
                    dve.wait_ge(a_pv, 2 * k + 2)
                    link(dve.tensor_tensor(den, small_a[:, k % 4, 1, :], small_a[:, k % 4, 3, :], ALU.add))
                    link(dve.reciprocal(den, den))
                    o4 = onorm_a[:, :].rearrange("p (e d) -> p e d", e=4)
                    link(dve.tensor_tensor(o4, ps[:, 6 + k % 2, 0:4 * AD].rearrange("p (e d) -> p e d", e=4),
                                           den.unsqueeze(2).to_broadcast([P, 4, AD]), ALU.mult))
                    gv = ga[:, i, :].rearrange("p (g c x) -> p c g x", g=AKV, c=2)[:, u]
                    dve.tensor_tensor(gv, onorm_a[:, :].rearrange("p (g x) -> p g x", g=AKV), gv, ALU.mult).then_inc(a_out, 1)

            for n in range(4 * NR, 5 * NR):
                split_lo(n)
            dve.wait_ge(c_sq, 2)
            invert(ss)
            invert(rstd)
            for t in range(TT):
                dve.tensor_scalar(cq[:, t, :], cq[:, t, :], ss[:, t:t + 1], None, ALU.mult).then_inc(c_norm, 1)
                dve.tensor_scalar(ckv[:, t, :], ckv[:, t, :], rstd[:, t:t + 1], None, ALU.mult).then_inc(c_norm, 1)
            dve.wait_ge(late_in, 48)
            H2 = BR // 2
            cosr, sinr = rope[:, 0, :, :], rope[:, 1, :, :]
            dve.tensor_tensor(krr[:, :, 0:H2], kr[:, :, 0:H2], cosr, ALU.mult)
            dve.tensor_tensor(krr[:, :, H2:], kr[:, :, H2:], cosr, ALU.mult)
            dve.tensor_tensor(kr2[:, :, 0:H2], kr[:, :, H2:], sinr, ALU.mult)
            link(dve.tensor_tensor(kr2[:, :, H2:], kr[:, :, 0:H2], sinr, ALU.mult))
            dve.tensor_tensor(krr[:, :, 0:H2], krr[:, :, 0:H2], kr2[:, :, 0:H2], ALU.subtract)
            dve.tensor_tensor(krr[:, :, H2:], krr[:, :, H2:], kr2[:, :, H2:], ALU.add).then_inc(kr_roped, 1)

            for n in range(5 * NR, 6 * NR - 1):
                split_lo(n)
            for t in range(TT):
                dve.wait_ge(gb_sig, t + 1)
                dve.tensor_tensor(gb[:, t, :], ps[:, t, :], gb[:, t, :], ALU.mult).then_inc(gb_done, 1)
            for n in range(6 * NR - 1, S_AB):
                split_lo(n)

            for n, (kind, a, hf) in enumerate(KUSES):
                b = n % 8
                cs = slice(hf * W, (hf + 1) * W)
                if kind == "v":
                    if a % 2 == 0:
                        dve.wait_ge(k_done, n + 1)
                        dve.tensor_copy(v_b[:, a, :], ps[:, b, :]).then_inc(k_free[b], 1)
                    continue
                dve.wait_ge(k_hi, K_SPLIT.index(n) + 1)
                if kind == "kr":
                    ins = dve.tensor_tensor(kT_l[BN:BQK, 0, cs], ps[0:BR, b, :], kT_h[BN:BQK, 0, cs].bitcast(f32), ALU.subtract)
                elif kind == "ckv":
                    ins = dve.tensor_tensor(ckvT_l[:, a, cs], ps[:, b, :], ckvT_h[:, a, cs].bitcast(f32), ALU.subtract)
                elif kind == "cq":
                    ins = dve.tensor_tensor(cqT_l[:, a, cs], ps[:, b, :], cqT_h[:, a, cs].bitcast(f32), ALU.subtract)
                else:
                    dve.tensor_tensor(kT_l[0:BN, 2 * a, cs], ps[0:BN, b, :], kT_h[0:BN, 2 * a, cs].bitcast(f32), ALU.subtract)
                    ins = dve.tensor_tensor(kT_l[0:BN, 2 * a + 1, cs], ps[BN:2 * BN, b, :],
                                            kT_h[0:BN, 2 * a + 1, cs].bitcast(f32), ALU.subtract)
                ins.then_inc(k_free[b], 1)

            dve.wait_ge(late_in, 64)
            for n in range(NU + LAG_PV):
                if n < NU:
                    kind, i, h = USES[n]
                    b0 = 2 * (n % 2)
                    if kind == "S":
                        m = SIDX[(i, h)]
                        dve.wait_ge(b_scores, n + 1)
                        if m >= 4:
                            dve.wait_ge(b_exp, m - 3)
                        dve.tensor_reduce(negm_b[:, m % 4:m % 4 + 1],
                                          ps[:, b0:b0 + 2, :].rearrange("p b c -> p (b c)")[:, 0:(i + 1) * P],
                                          AX.X, ALU.max, negate=True).then_inc(b_nmax, 1)
                        if i == TT - 1 and h < NR - 1:
                            split_lo(S_AB + h)
                    elif kind == "Q":
                        dve.wait_ge(q_out, i + 1)
                        if i >= 2:
                            dve.wait_ge(b_out, i - 1)
                        r = q_sb[:, i % 2, :].rearrange("p (h c) -> p h c", h=BH)
                        x1, x2 = r[:, :, BN:BN + H2], r[:, :, BN + H2:]
                        cb_, sb_ = (rope_b[:, e, i, :].unsqueeze(1).to_broadcast([P, BH, H2]) for e in range(2))
                        tmp = onorm_b[:, :].rearrange("p (e h c) -> p e h c", e=4, h=BH)
                        dve.tensor_tensor(tmp[:, 0], x1, sb_, ALU.mult)
                        dve.tensor_tensor(tmp[:, 1], x2, sb_, ALU.mult)
                        dve.tensor_tensor(tmp[:, 2], x1, cb_, ALU.mult)
                        link(dve.tensor_tensor(tmp[:, 3], x2, cb_, ALU.mult))
                        dve.tensor_tensor(x1, tmp[:, 2], tmp[:, 1], ALU.subtract)
                        dve.tensor_tensor(x2, tmp[:, 3], tmp[:, 0], ALU.add).then_inc(q_roped, 1)
                    else:
                        dve.wait_ge(qT_hi, i + 1)
                        dve.tensor_tensor(qT_l[0:BQK, i % 2, :, :], ps[0:BQK, b0:b0 + 2, :].rearrange("p b (h s) -> p (b h) s", h=4),
                                          qT_h[0:BQK, i % 2, :, :].bitcast(f32), ALU.subtract).then_inc(qT_lo, 1)
                if LAG_T <= n < NU + LAG_T and USES[n - LAG_T][0] == "S":
                    for m, t0, t1 in PIECES[USES[n - LAG_T][1:]]:
                        if m % 2 == 0:
                            dve.wait_ge(b_T, m + 1)
                            if m >= NPT:
                                dve.wait_ge(b_pv, m - NPT + 1)
                            dve.tensor_copy(pT_b[:, m % NPT, 0:(t1 - t0) * P], ps[:, 4, 0:(t1 - t0) * P]).then_inc(b_pT0, 1)
                if n >= LAG_PV and USES[n - LAG_PV][0] == "S" and USES[n - LAG_PV][2] == BH - 1:
                    i = USES[n - LAG_PV][1]
                    dve.wait_ge(b_pv, PIECES[(i, BH - 1)][-1][0] + 1)
                    dve.wait_ge(q_roped, min(TT, i + 2))
                    link(dve.reciprocal(rden_b[:, :], rs_b[:, i % 2, :]))
                    o8 = onorm_b[:, :].rearrange("p (h d) -> p h d", h=BH)
                    link(dve.tensor_tensor(o8, ps[:, 6 + i % 2, :].rearrange("p (h d) -> p h d", h=BH),
                                           rden_b[:, :].unsqueeze(2).to_broadcast([P, BH, BV]), ALU.mult))
                    dve.tensor_tensor(gb[:, i, :], onorm_b[:, :], gb[:, i, :], ALU.mult).then_inc(b_out, 1)

            def u_lo_out(m):
                br, t = m // TT, m % TT
                dve.wait_ge(u_hi, m + 1)
                cs = slice(t * P, (t + 1) * P)
                dve.tensor_tensor(uT_l[br][:, :, cs], ps[:, 6 + m % 2, :].rearrange("p (k s) -> p k s", k=KU),
                                  uT_h[br][:, :, cs].bitcast(f32), ALU.subtract).then_inc(u_lo, 1)

            def m_lo_out(t):
                for c in range(2):
                    dve.wait_ge(m_hi, 2 * t + c + 1)
                    ks = slice(4 * c, 4 * c + 4)
                    dve.tensor_tensor(mT_l[:, t % NMT, ks, :].rearrange("p k s -> p (k s)"), ps[:, 6 + c, :],
                                      mT_h[:, t % NMT, ks, :].rearrange("p k s -> p (k s)").bitcast(f32),
                                      ALU.subtract).then_inc(m_lo, 1)

            u_lo_out(0)
            u_lo_out(1)
            for n in range(4 * TT):
                if n + 2 < 2 * TT:
                    u_lo_out(n + 2)
                cb, t = (n // TT) % 2, n % TT
                dve.wait_ge(gate_in[n % NG], 16 * (n // NG + 1))
                dve.wait_ge(ab_done, n + 1)
                dst = merged[:, t, cb * W:(cb + 1) * W] if n < 2 * TT else gate[:, n % NG, :]
                dve.tensor_tensor(dst, ps[:, n % 6, :], gate[:, n % NG, :], ALU.mult).then_inc(ab_out, 1)
                if n == 1:
                    split_lo(S_AB + NR - 1)
                if n == TT:
                    for j in range(KU):
                        split_lo(S_AB + 2 * KU + j)
                if n == 2 * TT:
                    for j in range(KU):
                        split_lo(S_AB + 3 * KU + j)
                if n >= 2 * TT:
                    split_lo(S_WO + n - 2 * TT)
            m_lo_out(0)
            m_lo_out(1)
            dve.wait_ge(late_in, 80)
            for t in range(TT):
                if t + 2 < TT:
                    m_lo_out(t + 2)
                dve.wait_ge(o_sq, t + 1)
                invert(ss[:, t:t + 1])
                if t >= 2:
                    dve.wait_ge(stored[t % 2], 16 * (t // 2))
                b0 = 2 * (t % 3)
                dve.scalar_tensor_tensor(y_sb[:, t % 2, :], ps[:, b0:b0 + 2, :].rearrange("p b c -> p (b c)"),
                                         ss[:, t:t + 1], pg[:, :], ALU.mult, ALU.mult).then_inc(o_y, 1)

        @block.tensor
        def _(pe):
            mm = nc.tensor.matmul

            def product(out, l_h, l_l, r_h, r_l, first, last):
                mm(out, l_h, r_h, start=first, stop=False)
                mm(out, l_h, r_l, start=False, stop=False)
                return mm(out, l_l, r_h, start=False, stop=last)

            def turn(out, src):
                return nc.tensor.transpose(out, src, ident[0:src.shape[0], 0:src.shape[0]])

            def x_turn(t):
                pe.wait_ge(x_norm, t + 1)
                for c in range(2):
                    b = (2 * t + c) % 4
                    if t >= 2:
                        pe.wait_ge(hl_done, 2 * (t - 2) + c + 1)
                    for k in range(4):
                        ins = turn(ps[:, b, k * P:(k + 1) * P], x_sb[t][:, (4 * c + k) * P:(4 * c + k + 1) * P])
                    ins.then_inc(x_T, 1)

            def ka_turn(t):
                pe.wait_ge(kvc_out, t + 1)
                if t == 4:
                    pe.wait_ge(kz_lo, 2)
                ins = turn(ps[:, 7, (t % 4) * P:(t % 4 + 1) * P], ka[:, t, :])
                if t % 4 == 3:
                    ins.then_inc(ka_T, 1)

            def tokens_tile(t, k, blk, n, bank):
                s, cs = (blk * NR + k) % NR, slice(t * P, (t + 1) * P)
                return product(ps[:, bank, 0:n], hT_h[:, k, cs], hT_l[:, k, cs], w_h[:, s, 0:n], w_l[:, s, 0:n],
                               k == 0, k == KD - 1)

            pe.wait_ge(consts_in, 64)
            x_turn(0)
            for t in range(TT):
                if t + 1 < TT:
                    x_turn(t + 1)
                pe.wait_ge(hl_done, 2 * t + 2)
                if t >= 3:
                    pe.wait_ge(kvc_out, t - 2)
                for k in range(KD):
                    if t == 0:
                        pe.wait_ge(lo_done, k + 1)
                    ins = tokens_tile(t, k, 0, W, 4 + t % 3)
                    if k == KD - 1:
                        ins.then_inc(blk_done, 1)
                    elif t == TT - 1:
                        ins.then_inc(w_used, 1)
                if t >= 1:
                    ka_turn(t - 1)
            ka_turn(TT - 1)

            pe.wait_ge(hl_done, 2 * TT)
            for k in range(KD):
                s = NR + k
                pe.wait_ge(lo_done, s + 1)
                for b in range(8):
                    j, cs = b // 2, slice((b % 2) * W, (b % 2 + 1) * W)
                    if k == 0 and 4 <= b <= 6:
                        pe.wait_ge(kvc_out, TT)
                    if k == 0 and b == 7:
                        pe.wait_ge(kz_lo, 4)
                    ls = slice(j * P, (j + 1) * P)
                    ins = product(ps[:, b, :], w_h[:, k, ls], w_l[:, k, ls], hT_h[:, k, cs], hT_l[:, k, cs],
                                  k == 0, k == KD - 1)
                    if k == KD - 1:
                        ins.then_inc(blk_done, 1)
                if k < KD - 1:
                    ins.then_inc(w_used, 1)

            def tokens_block(blk, n, bank_free):
                for k in range(KD):
                    pe.wait_ge(lo_done, blk * NR + k + 1)
                    for t in range(TT):
                        if k == 0:
                            bank_free(t)
                        ins = tokens_tile(t, k, blk, n, t)
                        if k == KD - 1:
                            ins.then_inc(blk_done, 1)
                    if k < KD - 1:
                        ins.then_inc(w_used, 1)

            tokens_block(2, W, lambda t: pe.wait_ge(qa_lo, t + 1))

            pe.wait_ge(kz_lo, 4)
            for n in range(len(A_UNITS) + LAG_PV):
                if n < len(A_UNITS):
                    i, u = A_UNITS[n]
                    b0 = 2 * (n % 2)
                    if n < 2:
                        pe.wait_ge(ga_done, b0 + 2)
                    else:
                        pe.wait_ge(a_added, 2 * (n - 2) + 2)
                    qs = slice(i * P, (i + 1) * P)
                    ks = slice(0, P) if i == 0 else slice(i * P - CHUNK, (i + 1) * P)
                    width = ks.stop - ks.start
                    for g in range(AKV):
                        for e in range(2):
                            j = 2 * u + e
                            ins = product(ps[:, b0 + g, 2 * P * e:2 * P * e + width], qaT_h[:, j, qs], qaT_l[:, j, qs],
                                          kz_h[:, g, ks], kz_l[:, g, ks], True, True)
                    ins.then_inc(a_scores, 1)
                if LAG_T <= n < len(A_UNITS) + LAG_T:
                    k = n - LAG_T
                    i, u = A_UNITS[k]
                    pe.wait_ge(a_exp, k + 1)
                    for g in range(AKV):
                        m = 2 * k + g
                        if m < 2:
                            pe.wait_ge(ga_done, 4 + g + 1)
                        else:
                            pe.wait_ge((a_pT0, a_pT1)[g], k)
                        for e in range(2):
                            for c in range(0 if i else 1, 2):
                                ins = turn(ps[:, 4 + g, (2 * e + c) * P:(2 * e + c + 1) * P],
                                           s_a[:, k % NSA, 2 * g + e, c * P:(c + 1) * P])
                        ins.then_inc(a_T, 1)
                if n >= LAG_PV:
                    k = n - LAG_PV
                    i, u = A_UNITS[k]
                    if k < 2:
                        pe.wait_ge(ga_done, 6 + k + 1)
                    else:
                        pe.wait_ge(a_out, k - 1)
                    for g in range(AKV):
                        m = 2 * k + g
                        pe.wait_ge((a_pT0, a_pT1)[g], k + 1)
                        for e in range(2):
                            col = (2 * g + e) * AD
                            for c in range(0 if i else 1, 2):
                                ins = mm(ps[:, 6 + k % 2, col:col + AD], pT_a[:, m % NPA, (2 * e + c) * P:(2 * e + c + 1) * P],
                                         va[:, i - 1 + c, g * AD:(g + 1) * AD], start=(c == (0 if i else 1)), stop=(c == 1))
                        ins.then_inc(a_pv, 1)

            def after_a(t):
                if t < 4:
                    pe.wait_ge(a_added, 2 * len(A_UNITS))
                elif t < 6:
                    pe.wait_ge((a_pT0, a_pT1)[t - 4], len(A_UNITS))
                else:
                    pe.wait_ge(a_out, len(A_UNITS))

            tokens_block(3, QL + BR, after_a)
            tokens_block(4, W, lambda t: pe.wait_ge(cq_out, t + 1))
            for b in range(4):
                tokens_block(5 + b, W, lambda t: pe.wait_ge(gb_done, t + 1) if b == 0 else pe.wait_ge(gm_out, (b - 1) * TT + t + 1))

            pe.wait_ge(kr_roped, 1)
            pe.wait_ge(c_norm, 2 * TT)
            k_release = [0] * 8
            for n, (kind, a, hf) in enumerate(KUSES):
                b = n % 8
                if n < 8:
                    pe.wait_ge(gm_out, 3 * TT + b + 1)
                else:
                    pe.wait_ge(k_free[b], n // 8)
                cs = slice(hf * W, (hf + 1) * W)
                if kind in ("kr", "ckv", "cq"):
                    for j in range(4):
                        t = 4 * hf + j
                        src = {"kr": krr, "ckv": ckv, "cq": cq}[kind]
                        if kind == "kr":
                            ins = turn(ps[0:BR, b, j * P:(j + 1) * P], src[:, t, :])
                        else:
                            ins = turn(ps[:, b, j * P:(j + 1) * P], src[:, t, a * P:(a + 1) * P])
                elif kind == "v":
                    if a == 0:
                        pe.wait_ge(lo_done, S_UV + KK)
                    for c in range(KK):
                        pe.wait_ge(k_free[(KR_N + (a // 4) * KK + c) % 8], 1)
                    ts = slice(a * P, (a + 1) * P)
                    for k in range(KK):
                        ins = product(ps[:, b, :], ckvT_h[:, k, ts], ckvT_l[:, k, ts], wv_h[:, k, :], wv_l[:, k, :],
                                      k == 0, k == KK - 1)
                else:
                    if a == 0:
                        pe.wait_ge(lo_done, S_AB)
                    ls = slice(a * P, (a + 1) * P)
                    for k in range(KK):
                        ins = product(ps[:, b, :], wk_h[:, k, ls], wk_l[:, k, ls], ckvT_h[:, k, cs], ckvT_l[:, k, cs],
                                      k == 0, k == KK - 1)
                ins.then_inc(k_done, 1)

            for b in range(8):
                pe.wait_ge(k_free[b], (len(KUSES) - b + 7) // 8)
            released = [0, 0]
            for n in range(NU + LAG_PV):
                if n < NU:
                    kind, i, h = USES[n]
                    b0 = 2 * (n % 2)
                    if n >= 2:
                        pk, pi, ph = USES[n - 2]
                        if pk == "S":
                            pe.wait_ge(b_exp, SIDX[(pi, ph)] + 1)
                        elif pk == "Q":
                            pe.wait_ge(q_out, pi + 1)
                        else:
                            pe.wait_ge(qT_lo, pi + 1)
                    if kind == "Q":
                        ts = slice(i * P, (i + 1) * P)
                        for c0, c1, b in ((0, W, b0), (W, BH * BQK, b0 + 1)):
                            for k in range(KQ):
                                ins = product(ps[:, b, 0:c1 - c0], cqT_h[:, k, ts], cqT_l[:, k, ts],
                                              wuq_h[:, k, c0:c1], wuq_l[:, k, c0:c1], k == 0, k == KQ - 1)
                    elif kind == "QT":
                        pe.wait_ge(q_roped, i + 1)
                        for hh in range(BH):
                            ins = turn(ps[0:BQK, b0 + hh // 4, (hh % 4) * P:(hh % 4 + 1) * P],
                                       q_sb[:, i % 2, hh * BQK:(hh + 1) * BQK])
                    else:
                        if h == 0:
                            pe.wait_ge(qT_lo, i + 1)
                        if (i, h) == (0, 0):
                            pe.wait_ge(mask_rows, 3)
                            pe.wait_ge(kr_spread, 4)
                            pe.wait_ge(qmask_rows, 6)
                        a = i % 2
                        for t0 in range(0, i, 4):
                            t1 = min(i, t0 + 4)
                            ks = slice(t0 * P, t1 * P)
                            product(ps[:, b0 + t0 // 4, 0:(t1 - t0) * P], qT_h[0:BQK, a, h, :], qT_l[0:BQK, a, h, :],
                                    kT_h[0:BQK, h, ks], kT_l[0:BQK, h, ks], True, True)
                        ks = slice(i * P, (i + 1) * P)
                        ins = product(ps[:, b0 + i // 4, (i % 4) * P:(i % 4 + 1) * P], qT_h[0:BQK + 1, a, h, :],
                                      qT_l[0:BQK + 1, a, h, :], kT_h[0:BQK + 1, h, ks], kT_l[0:BQK + 1, h, ks], True, True)
                    ins.then_inc(b_scores, 1)
                if LAG_T <= n < NU + LAG_T and USES[n - LAG_T][0] == "S":
                    _, i, h = USES[n - LAG_T]
                    pe.wait_ge(b_exp, SIDX[(i, h)] + 1)
                    for m, t0, t1 in PIECES[(i, h)]:
                        if m >= 2:
                            pe.wait_ge((b_pT0, b_pT1)[m % 2], m // 2)
                        for t in range(t0, t1):
                            ins = turn(ps[:, 4 + m % 2, (t - t0) * P:(t - t0 + 1) * P],
                                       p_b[:, SIDX[(i, h)] % NPB, t * P:(t + 1) * P])
                        ins.then_inc(b_T, 1)
                if n >= LAG_PV and USES[n - LAG_PV][0] == "S":
                    _, i, h = USES[n - LAG_PV]
                    if h == 0 and i >= 2:
                        pe.wait_ge(b_out, i - 1)
                    for m, t0, t1 in PIECES[(i, h)]:
                        pe.wait_ge((b_pT0, b_pT1)[m % 2], m // 2 + 1)
                        for t in range(t0, t1):
                            ins = mm(ps[:, 6 + i % 2, h * BV:(h + 1) * BV], pT_b[:, m % NPT, (t - t0) * P:(t - t0 + 1) * P],
                                     v_b[:, t, h * BV:(h + 1) * BV], start=(t == 0), stop=(t == i))
                        ins.then_inc(b_pv, 1)

            def u_turn(m):
                br, t = m // TT, m % TT
                if m == 0:
                    pe.wait_ge(b_out, TT - 1)
                if m == 1:
                    pe.wait_ge(b_out, TT)
                if m >= 2:
                    pe.wait_ge(u_lo, m - 1)
                for k in range(KU):
                    ins = turn(ps[:, 6 + m % 2, k * P:(k + 1) * P], (ga, gb)[br][:, t, k * P:(k + 1) * P])
                ins.then_inc(u_T, 1)

            u_turn(0)
            u_turn(1)
            for n in range(4 * TT):
                if n + 2 < 2 * TT:
                    u_turn(n + 2)
                blk, t = n // TT, n % TT
                br, s0, cs = blk // 2, (blk % 2) * KU, slice(t * P, (t + 1) * P)
                if n == 0:
                    pe.wait_ge(b_exp, len(SIDX))
                    pe.wait_ge(b_pT0, (npiece + 1) // 2)
                    pe.wait_ge(b_pT1, npiece // 2)
                if n >= 6:
                    pe.wait_ge(ab_out, n - 5)
                pe.wait_ge(u_lo, br * TT + t + 1)
                if t == 0:
                    pe.wait_ge(lo_done, S_AB + (blk + 1) * KU)
                for k in range(KU):
                    ins = product(ps[:, n % 6, :], uT_h[br][:, k, cs], uT_l[br][:, k, cs],
                                  w_h[:, s0 + k, :], w_l[:, s0 + k, :], k == 0, k == KU - 1)
                ins.then_inc(ab_done, 1)

            def m_turn(t):
                pe.wait_ge(g_add, TT + t + 1)
                for c in range(2):
                    if t == 0:
                        pe.wait_ge(u_lo, 2 * TT)
                    else:
                        pe.wait_ge(m_lo, 2 * (t - 1) + c + 1)
                    for k in range(4):
                        ins = turn(ps[:, 6 + c, k * P:(k + 1) * P], merged[:, t, (4 * c + k) * P:(4 * c + k + 1) * P])
                    ins.then_inc(m_T, 1)

            m_turn(0)
            m_turn(1)
            pe.wait_ge(ab_out, 4 * TT)
            pe.wait_ge(lo_done, NS)
            for t in range(TT):
                if t + 2 < TT:
                    m_turn(t + 2)
                if t >= 3:
                    pe.wait_ge(o_y, t - 2)
                pe.wait_ge(m_lo, 2 * t + 2)
                for cb in range(2):
                    for k in range(KD):
                        ins = product(ps[:, 2 * (t % 3) + cb, :], mT_h[:, t % NMT, k, :], mT_l[:, t % NMT, k, :],
                                      wo_h[2 * k + cb][:, :], wo_l[2 * k + cb][:, :], k == 0, k == KD - 1)
                ins.then_inc(o_done, 1)


_INS = ["x", "pre_norm_g", "w_in", "a_sinks", "b_q_norm_g", "b_w_uq", "b_kv_norm_g", "b_w_ukv",
        "a_w_o", "b_w_o", "w_out", "post_norm_g"]


def kernel(**inputs):
    import concourse.bacc as bacc
    from concourse.bass_utils import run_bass_kernel_spmd

    nc = bacc.Bacc("TRN2", target_bir_lowering=False, num_devices=1)
    arrays, args = {}, []
    feeds = [(n, np.ascontiguousarray(np.asarray(inputs[n])[0])) for n in _INS]
    feeds = [(n, np.ascontiguousarray(a.reshape(-1, P).T) if n in ("pre_norm_g", "b_q_norm_g", "b_kv_norm_g") else a)
             for n, a in feeds]
    feeds += [("ident", np.eye(P, dtype=np.float32)), ("rope", rope_table()), ("alibi", alibi_table())]
    for name, a in feeds:
        arrays[f"in_{name}"] = a
        args.append(nc.dram_tensor(f"in_{name}", a.shape, mybir.dt.from_np(a.dtype), kind="ExternalInput").ap())
    out = nc.dram_tensor("out", (SEQ, DM), mybir.dt.float32, kind="ExternalOutput").ap()
    build(nc, *args, out)
    r = run_bass_kernel_spmd(nc, [arrays], core_ids=[0])
    return r.results[0]["out"].reshape(1, SEQ, DM)
```

```python
import numpy as np
import concourse.bass as bass
from concourse import mybir
from contextlib import ExitStack

P = 128
SEQ, DM = 1024, 1024
CHUNK = 64
AH, AKV, AD = 8, 2, 64
AG = AH // AKV
BH, BN, BR, BV = 8, 64, 32, 64
BQK = BN + BR
QL, KL = 384, 256
W = 512
TT = SEQ // P
KD = DM // P
KQ, KK, KU = QL // P, KL // P, W // P
EPS = 1e-6
NEG = -1e30
THETA = 10000.0

C_QA = 0
C_KA = C_QA + AH * AD
C_VA = C_KA + AKV * AD
C_GA = C_VA + AKV * AD
C_CQ = C_GA + AH * AD
C_CKV = C_CQ + QL
C_KR = C_CKV + KL
C_GB = C_KR + BR
C_GM = C_GB + BH * BV
IN_TOTAL = C_GM + 2 * DM


def rope_table():
    inv = (1.0 / (np.float32(THETA) ** (np.arange(0, BR, 2, dtype=np.float32) / np.float32(BR)))).astype(np.float32)
    ang = (np.arange(SEQ, dtype=np.float32)[:, None] * inv[None, :]).astype(np.float32)
    cos, sin = np.cos(ang).astype(np.float32), np.sin(ang).astype(np.float32)
    return np.ascontiguousarray(np.stack([cos, sin]).reshape(2, TT, P, BR // 2).transpose(2, 0, 1, 3))


def alibi_table():
    q = np.arange(CHUNK)[:, None] + CHUNK
    k = np.arange(2 * CHUNK)[None, :]
    dist = np.abs(q - k).astype(np.float32)
    slopes = [np.float32(2.0 ** (-8.0 * (h + 1) / AH)) for h in range(AH)]
    t = np.stack([-s * dist for s in slopes]).astype(np.float32)
    return np.ascontiguousarray(t.reshape(AH // 2, 2, CHUNK, P).transpose(1, 2, 0, 3).reshape(P, AH // 2, P))


def mask_rows():
    m = np.zeros((2, TT, P), np.float32)
    for t in range(TT):
        m[t % 2, t, CHUNK:] = 1.0
    return m.reshape(2, SEQ)


def build(nc, x_d, pre_g_d, w_in_d, sinks_d, qg_d, w_uq_d, kvg_d, w_ukv_d, a_wo_d, b_wo_d,
          w_out_d, post_g_d, ident_d, rope_d, alibi_d, mask_d, out_d):
    f32, f32r = mybir.dt.float32, mybir.dt.float32r
    ALU, ACT, AX = mybir.AluOpType, mybir.ActivationFunctionType, mybir.AxisListType
    KB = 1024
    BASE = 16512

    def at(name, shape, dt, kb):
        return nc.alloc_sbuf_tensor_at(name, shape, dt, offset=BASE + int(kb * KB))

    hT_h, hT_l = at("hT_h", [P, KD, SEQ], f32r, 0), at("hT_l", [P, KD, SEQ], f32r, 32)
    kT_h, kT_l = at("kT_h", [P, BH, SEQ], f32r, 0), at("kT_l", [P, BH, SEQ], f32r, 32)
    wv_h, wv_l = at("wv_h", [P, KK, W], f32r, 56), at("wv_l", [P, KK, W], f32r, 60)
    uT_h = [at("uaT_h", [P, KU, SEQ], f32r, 0), at("ubT_h", [P, KU, SEQ], f32r, 32)]
    uT_l = [at("uaT_l", [P, KU, SEQ], f32r, 16), at("ubT_l", [P, KU, SEQ], f32r, 48)]
    NMT = 3
    mT_h, mT_l = at("mT_h", [P, NMT, KD, P], f32r, 0), at("mT_l", [P, NMT, KD, P], f32r, 12)
    xres = at("xres", [P, 2, DM], f32, 24)
    NR = 8
    w_h, w_l = at("w_h", [P, NR, W], f32r, 64), at("w_l", [P, NR, W], f32r, 80)
    cqT_h, cqT_l = at("cqT_h", [P, KQ, SEQ], f32r, 64), at("cqT_l", [P, KQ, SEQ], f32r, 76)
    wk_h, wk_l = at("wk_h", [P, KK, W], f32r, 136), at("wk_l", [P, KK, W], f32r, 140)
    q_sb = at("q_sb", [P, 2, BH * BQK], f32, 88)
    onorm_b = at("onorm_b", [P, BH * BV], f32, 94)
    y_sb = at("y_sb", [P, 2, DM], f32, 64)
    pg = at("pg", [P, DM], f32, 80)
    junk_y = at("junk_y", [P, DM], f32, 84)
    NRAW = 4
    raw = at("raw", [P, NRAW, W], f32, 96)
    ga, gb = at("ga", [P, TT, W], f32, 104), at("gb", [P, TT, W], f32, 120)
    x_sb = [at(f"x_sb{t}", [P, DM], f32, (157 + 4 * t) if t < 4 else (104 + 4 * (t - 4))) for t in range(TT)]
    junk_x = at("junk_x", [P, DM], f32, 120)
    qaT = at("qaT", [P, SEQ // CHUNK, AG, CHUNK], f32, 120)
    NPA = 3
    pT_a = at("pT_a", [P, NPA, W], f32, 157)
    alibi = at("alibi", [P, AH // 2, P], f32, 163)
    onorm_a = at("onorm_a", [P, 2, W], f32, 165)
    cq = at("cq", [P, TT, QL], f32, 136)
    ckv = at("ckv", [P, TT, KL], f32, 149)
    NPB, NPT = 3, 4
    p_b = at("p_b", [P, NPB, SEQ], f32, 136)
    pT_b = at("pT_b", [P, NPT, W], f32, 148)
    v_b = at("v_b", [P, TT, BH * BV], f32, 157)
    merged = at("merged", [P, TT, DM], f32, 157)
    kz = at("kz", [P, AKV, SEQ], f32, 173)
    NST = 4
    stage = at("stage", [P, NST, W], f32, 157)
    kr = at("kr", [P, TT, BR], f32, 181)
    krr = at("krr", [P, TT, BR], f32, 182)
    kr2 = at("kr2", [P, TT, BR], f32, 183)
    junk_c = at("junk_c", [P, QL], f32, 184)
    ckvT_h, ckvT_l = at("ckvT_h", [P, 2, KK, W], f32r, 173), at("ckvT_l", [P, 2, KK, W], f32r, 181)
    qT_h, qT_l = at("qT_h", [P, 2, BH, P], f32r, 173), at("qT_l", [P, 2, BH, P], f32r, 181)
    va = at("va", [P, TT, AKV * AD], f32, 189)
    va_s = at("va_s", [P, TT, AKV * AD], f32, 199)
    NSA = 3
    s_a = at("s_a", [P, NSA, AH // 2, P], f32, 193)
    ka = at("ka", [P, TT, AKV * AD], f32, 193)
    NSM = 6
    small_a = at("small_a", [P, NSM, 5, AH // 2], f32, 205)
    wuq_h, wuq_l = at("wuq_h", [P, KQ, BH * BQK], f32r, 189), at("wuq_l", [P, KQ, BH * BQK], f32r, 198)
    NG = 3
    gate = at("gate", [P, NG, W], f32, 201)
    wo_at = [104 + 4 * j for j in range(13)] + [189 + 4 * j for j in range(3)]
    wo_h = [at(f"wo_h{j}", [P, W], f32r, kb) for j, kb in enumerate(wo_at)]
    wo_l = [at(f"wo_l{j}", [P, W], f32r, kb + 2) for j, kb in enumerate(wo_at)]
    ident = at("ident", [P, P], f32, 207)
    stats = at("stats", [P, 64], f32, 207.5)
    rope = at("rope", [P, 2, TT, BR // 2], f32, 186)
    rope_b = at("rope_b", [P, 2, TT, BR // 2], f32, 156)
    ss, rstd = stats[:, 0:8], stats[:, 8:16]
    g_pre, g_q, g_kv = stats[:, 16:24], stats[:, 24:27], stats[:, 27:29]
    sink, nsink = stats[:, 32:36], stats[:, 40:44]
    rs_b = stats[:, 48:64].rearrange("p (a h) -> p a h", a=2)
    negm_b = at("negm_b", [P, 4], f32, 207.75)
    rden_b = at("rden_b", [P, 8], f32, 207.78125)

    eps = at("eps", [P, 1], f32, 207.8125)

    gates_dram = nc.dram_tensor("gates_dram", (4 * TT, P, W), f32, kind="Internal").ap()

    ctx = ExitStack()
    with ctx:
        ps = ctx.enter_context(nc.psum_tensor("ps", [P, 8, W], f32))

        def sem(name):
            return ctx.enter_context(nc.semaphore(name))

        slices = []
        NKB, K_BANK = 6, 2

        def add_slice(loads, n, g, hi, lo, slot=None):
            slices.append(dict(loads=loads, n=n, g=g, hi=hi, lo=lo, slot=slot))

        def rows(m, k):
            return m[k * P:(k + 1) * P, :]

        def ring_slice(loads, n, g):
            s = len(slices) % NR
            add_slice(loads, n, g, w_h[:, s, 0:n], w_l[:, s, 0:n], s)

        def in_slice(k, c0, n):
            ring_slice([((0, n), rows(w_in_d, k)[:, c0:c0 + n])], n, g_pre[:, k:k + 1])

        for k in range(KD):
            r = rows(w_in_d, k)
            ring_slice([((0, 256), r[:, C_KA:C_GA]), ((256, 512), r[:, C_CKV:C_KR])], W, g_pre[:, k:k + 1])
        for k in range(KD):
            r = rows(w_in_d, k)
            ring_slice([(("pair", g), r[:, C_QA + g * 256:C_QA + (g + 1) * 256].rearrange("p (j d) -> p j d", d=AD))
                        for g in range(AKV)], W, g_pre[:, k:k + 1])
        for k in range(KD):
            in_slice(k, C_GA, W)
        for k in range(KD):
            r = rows(w_in_d, k)
            ring_slice([((0, QL), r[:, C_CQ:C_CKV]), ((QL, QL + BR), r[:, C_KR:C_GB])], QL + BR, g_pre[:, k:k + 1])
        for k in range(KD):
            in_slice(k, C_GB, W)
        for b in range(4):
            for k in range(KD):
                in_slice(k, C_GM + b * W, W)
        S_UQ = len(slices)
        for k in range(KQ):
            for c in range(2):
                cs = slice(c * QL, (c + 1) * QL)
                add_slice([((0, QL), rows(w_uq_d, k)[:, cs])], QL, g_q[:, k:k + 1], wuq_h[:, k, cs], wuq_l[:, k, cs])
        S_UV = len(slices)
        for part, hi, lo in ((BN, wv_h, wv_l), (0, wk_h, wk_l)):
            for k in range(KK):
                src = rows(w_ukv_d, k).rearrange("p (h c) -> p h c", h=BH)[:, :, part:part + BN]
                add_slice([("heads", src)], W, g_kv[:, k:k + 1], hi[:, k, :], lo[:, k, :])
        S_AB = len(slices)
        for m, cb in ((a_wo_d, 0), (a_wo_d, 1), (b_wo_d, 0), (b_wo_d, 1)):
            for k in range(KU):
                s = (len(slices) - S_AB) % NR
                add_slice([((0, W), rows(m, k)[:, cb * W:(cb + 1) * W])], W, None, w_h[:, s, :], w_l[:, s, :], s)
        S_WO = len(slices)
        for j in range(2 * KD):
            k, cb = j // 2, j % 2
            add_slice([((0, W), rows(w_out_d, k)[:, cb * W:(cb + 1) * W])], W, None, wo_h[j][:, :], wo_l[j][:, :])
        NS = len(slices)
        raw_total = []
        filled = [0] * NRAW
        for n, s in enumerate(slices):
            filled[n % NRAW] += 16 * len(s["loads"])
            raw_total.append(filled[n % NRAW])

        raw_in = [sem(f"raw_in{r}") for r in range(NRAW)]
        hi_done, lo_done = sem("hi_done"), sem("lo_done")
        w_used = sem("w_used")
        consts_in = sem("consts_in")
        late_in = sem("late_in")
        x_in = [sem(f"x_in{t}") for t in range(TT)]
        x_sq, x_norm, x_T, hh_done, hl_done = (sem(n) for n in ("x_sq", "x_norm", "x_T", "hh_done", "hl_done"))
        blk_done = sem("blk_done")
        kvc_out = sem("kvc_out")
        ka_T, kz_out, kz_zero = (sem(n) for n in ("ka_T", "kz_out", "kz_zero"))
        qa_out = [sem("qa_out0"), sem("qa_out1")]
        ga_sig, ga_done, gb_sig, gb_done = (sem(n) for n in ("ga_sig", "ga_done", "gb_sig", "gb_done"))
        a_scores, a_added, a_nmax, a_exp, a_T, a_pT, a_pv, a_norm, a_out = (
            sem("a_" + n) for n in ("scores", "added", "nmax", "exp", "T", "pT", "pv", "norm", "out"))
        first_zero = sem("first_zero")
        cq_out, c_sq, c_norm, kr_roped = (sem(n) for n in ("cq_out", "c_sq", "c_norm", "kr_roped"))
        gm_out = sem("gm_out")
        gm_stored = [sem(f"gm_stored{i}") for i in range(NST)]
        k_done, k_hi = sem("k_done"), sem("k_hi")
        k_free = [sem(f"k_free{b}") for b in range(NKB)]
        kr_spread = sem("kr_spread")
        rope_in = sem("rope_in")
        mask_in, mask_q, mask_k = sem("mask_in"), sem("mask_q"), sem("mask_k")
        b_scores, b_nmax, b_exp, b_T, b_pT0, b_pT1, b_pv, b_out = (
            sem("b_" + n) for n in ("scores", "nmax", "exp", "T", "pT0", "pT1", "pv", "out"))
        b_free = [sem("b_free0"), sem("b_free1")]
        q_out, q_roped, qT_hi, qT_lo = (sem(n) for n in ("q_out", "q_roped", "qT_hi", "qT_lo"))
        u_T, u_hi, u_lo = sem("u_T"), sem("u_hi"), sem("u_lo")
        ab_done, ab_out, g_add = sem("ab_done"), sem("ab_out"), sem("g_add")
        gate_in = [sem(f"gate_in{i}") for i in range(NG)]
        m_T, m_hi, m_lo = sem("m_T"), sem("m_hi"), sem("m_lo")
        o_done, o_sq, o_y, o_add0, o_add1 = (sem(n) for n in ("o_done", "o_sq", "o_y", "o_add0", "o_add1"))
        xres_in = [sem("xres_in0"), sem("xres_in1")]
        stored = [sem("stored0"), sem("stored1")]
        eps_set = sem("eps_set")
        dve_step, act_step = sem("dve_step"), sem("act_step")

        M_EARLY = (28, 30)
        NB0, NB = TT, 8 * 9
        NCH = SEQ // CHUNK
        USES = [("Q", 0, 0), ("QT", 0, 0)]
        for i in range(TT):
            for h in range(BH):
                USES.append(("S", i, h))
                if i + 1 < TT and h == 1:
                    USES.append(("Q", i + 1, 0))
                if i + 1 < TT and h == 5:
                    USES.append(("QT", i + 1, 0))
        PIECES = {}
        SIDX = {}
        npiece = 0
        pt_evacs = [0, 0]
        for n, (kind, i, h) in enumerate(USES):
            if kind != "S":
                continue
            SIDX[(i, h)] = len(SIDX)
            PIECES[(i, h)] = []
            for t0 in range(0, i + 1, 4):
                PIECES[(i, h)].append((npiece, t0, min(i + 1, t0 + 4)))
                npiece += 1
        LAG, LAG_V, LAG_N = 3, 4, 5
        A_SB, A_TB, A_OB = 2, 4, 6
        A_STEPS = NCH + LAG_V

        def filler(n):
            if not 0 <= n < A_STEPS:
                return []
            return [divmod(u, KD) for u in range(TT * KD * n // A_STEPS, TT * KD * (n + 1) // A_STEPS)]
        NU = len(USES)
        ROPE_LAG = 3

        def queries_of(n, late):
            if 1 < n < NU and USES[n][0] == "Q" and (USES[n][1] <= 4) == late:
                return USES[n][1]
            return None
        SB, BEFORE, last, pos = [], [], {}, 0
        for n, (kind, i, h) in enumerate(USES):
            two = kind != "S" or i >= 4
            if two:
                pos += pos % 2
            if n == 1:
                pos = 0
            banks = [pos % 4, pos % 4 + 1] if two else [pos % 4]
            SB.append(banks[0])
            BEFORE.append(sorted({last[b] for b in banks if b in last}))
            for b in banks:
                last[b] = n
            pos += len(banks)

        KUSES = [("kr", 0, 0), ("kr", 0, 1)] + [("ckv", k, hf) for hf in range(2) for k in range(KK)]
        N_CKV = len(KUSES)
        cqs = [("cq", k, hf) for hf in range(2) for k in range(KQ)]
        for t in range(TT):
            KUSES += [("v", t, 0)] + cqs[t:t + 1]
        N_V = len(KUSES)
        N_Q = KUSES.index(("v", TT - 1, 0))
        N_CQ = KUSES.index(cqs[-1]) + 1
        KUSES += [("kn", pr, hf) for hf in range(2) for pr in range(BH // 2)]
        N_QT = KUSES.index(("kn", 0, 1))
        NK = len(KUSES)
        K_LAST = [(NK - b + NKB - 1) // NKB for b in range(NKB)]
        K_SPLIT = [n for n, u in enumerate(KUSES) if u[0] != "v"]

        def span(b0, n):
            nb = (n + W - 1) // W
            return ps[:, b0:b0 + nb, :].rearrange("p b c -> p (b c)")[:, 0:n]

        block = ctx.enter_context(nc.Block())

        @block.sync
        def _(sp):
            def load_x(t):
                sp.dma_start(x_sb[t][:, :], x_d[t * P:(t + 1) * P, :]).then_inc(x_in[t], 16)

            def load_slice(n):
                if n >= NRAW:
                    sp.wait_ge(lo_done, n - NRAW + 1)
                slot = raw[:, n % NRAW, :]
                for where, src in slices[n]["loads"]:
                    if where == "heads":
                        dst = slot.rearrange("p (h d) -> p h d", h=BH)
                    elif where[0] == "pair":
                        dst = slot.rearrange("p (j g d) -> p j g d", j=AG, g=AKV)[:, :, where[1], :]
                    else:
                        dst = slot[:, where[0]:where[1]]
                    sp.dma_start(dst, src).then_inc(raw_in[n % NRAW], 16)

            load_x(0)
            x_after = {3: (1,), 7: (2,), 8: (3,), 9: (4,), 10: (5,), 11: (6, 7)}
            for n in range(NS):
                load_slice(n)
                for t in x_after.get(n, ()):
                    load_x(t)
            for t in range(TT):
                for c, added in enumerate((o_add0, o_add1)):
                    cs = slice(c * W, (c + 1) * W)
                    sp.wait_ge(added, t + 1)
                    sp.dma_start(out_d[t * P:(t + 1) * P, cs], y_sb[:, t % 2, cs]).then_inc(stored[t % 2], 16)
            for r in range(2):
                sp.wait_ge(stored[r], 2 * 16 * (TT // 2))

        @block.gpsimd
        def _(pool):
            pool.dma_start(ident[:, :], ident_d).then_inc(consts_in, 16)
            pool.dma_start(g_pre, pre_g_d).then_inc(consts_in, 16)
            pool.dma_start(g_q, qg_d).then_inc(consts_in, 16)
            pool.dma_start(g_kv, kvg_d).then_inc(consts_in, 16)
            for e in range(2):
                pool.dma_start(sink[CHUNK * e:CHUNK * (e + 1), :], sinks_d[e].partition_broadcast(CHUNK)).then_inc(late_in, 16)
            pool.memset(kz[64:128, 0, :], 0.0).then_inc(kz_zero, 1)
            pool.memset(kz[0:64, 1, :], 0.0).then_inc(kz_zero, 1)
            pool.wait_ge(x_T, 2 * 4)
            pool.dma_start(alibi[:, :, :], alibi_d).then_inc(late_in, 16)
            pool.memset(va_s[0:CHUNK, 0, :], 0.0).then_inc(first_zero, 1)
            pool.wait_ge(ka_T, 2)
            pool.memset(s_a[:, 0, :, 0:CHUNK], 0.0).then_inc(first_zero, 1)
            for i in range(TT):
                pool.wait_ge(a_norm, 2 * i + 2)
                pool.tensor_tensor(ga[:, i, :], onorm_a[:, i % 2, :], ga[:, i, :], ALU.mult).then_inc(a_out, 1)
            pool.dma_start(rope[:, :, :, :], rope_d).then_inc(rope_in, 16)
            for n in range(4 * TT):
                pool.wait_ge(gm_out, n + 1)
                pool.dma_start(gates_dram[n], stage[:, n % NST, :]).then_inc(gm_stored[n % NST], 16)
            pool.wait_ge(blk_done, NB)
            pool.dma_start(kT_h[BQK:BQK + 2, :, :], mask_d.unsqueeze(1).to_broadcast([2, BH, SEQ])).then_inc(mask_in, 16)
            pool.wait_ge(k_done, N_CKV)
            pool.dma_start(rope_b[:, :, :, :], rope_d).then_inc(rope_in, 16)
            for b in range(2):
                pool.wait_ge(k_free[b], 1)

            def spread(kT, h0, h1):
                pool.dma_start(kT[BN:BQK, h0:h1, :], kT[BN:BQK, 0:1, :].to_broadcast([BR, h1 - h0, SEQ])).then_inc(kr_spread, 16)

            spread(kT_h, 1, BH)
            spread(kT_l, 1, BH - 2)
            pool.wait_ge(k_done, N_V)
            spread(kT_l, BH - 2, BH)
            pool.wait_ge(k_done, N_QT)
            pool.memset(qT_h[BQK:BQK + 2, 0, :, :].bitcast(f32), 0.0).then_inc(mask_q, 1)
            pool.wait_ge(mask_q, 1)
            pool.memset(qT_h[BQK:BQK + 1, 0, :, 0:CHUNK].bitcast(f32), NEG).then_inc(mask_q, 1)
            pool.wait_ge(k_done, NK)
            pool.memset(qT_h[BQK:BQK + 2, 1, :, :].bitcast(f32), 0.0).then_inc(mask_q, 1)
            pool.wait_ge(mask_q, 3)
            pool.memset(qT_h[BQK:BQK + 2, 1, :, 0:CHUNK].bitcast(f32), NEG).then_inc(mask_q, 1)
            pool.wait_ge(mask_q, 4)
            pool.memset(qT_h[BQK:BQK + 1, 1, :, 0:CHUNK].bitcast(f32), 0.0).then_inc(mask_q, 1)
            pool.wait_ge(mask_in, 16)
            for t in range(TT - 2):
                for h in range(BH):
                    pool.wait_ge(b_scores, USES.index(("S", t + 1, h)) + 1)
                    pool.memset(kT_h[BQK:BQK + 2, h, t * P + CHUNK:(t + 1) * P].bitcast(f32), 0.0).then_inc(mask_k, 1)
            for i in range(NST):
                pool.wait_ge(gm_stored[i], 16 * (4 * TT // NST))
            pool.wait_ge(q_out, TT)
            for n in range(4 * TT + NG):
                if n >= NG and n - NG >= 2 * TT:
                    m = n - NG
                    cb, t = (m // TT) % 2, m % TT
                    pool.wait_ge(ab_out, m + 1)
                    dst = merged[:, t, cb * W:(cb + 1) * W]
                    pool.tensor_tensor(dst, dst, gate[:, m % NG, :], ALU.add).then_inc(g_add, 1)
                if n < 4 * TT:
                    if n >= NG:
                        pool.wait_ge(ab_out, n - NG + 1)
                    if n - NG >= 2 * TT:
                        pool.wait_ge(g_add, n - NG - 2 * TT + 1)
                    pool.dma_start(gate[:, n % NG, :], gates_dram[n]).then_inc(gate_in[n % NG], 16)
                if n in (2 * TT + 4, 2 * TT + 6):
                    r = (n - 2 * TT - 4) // 2
                    pool.dma_start(xres[:, r, :], x_d[r * P:(r + 1) * P, :]).then_inc(xres_in[r], 16)
            pool.wait_ge(ab_done, 4 * TT)
            pool.dma_start(pg[:, :], post_g_d.partition_broadcast(P)).then_inc(late_in, 16)
            for t in range(TT):
                pool.wait_ge(o_y, 2 * t + 1)
                pool.wait_ge(xres_in[t % 2], 16 * (t // 2 + 1))
                pool.tensor_tensor(y_sb[:, t % 2, 0:W], y_sb[:, t % 2, 0:W], xres[:, t % 2, 0:W], ALU.add).then_inc(o_add0, 1)
                if t + 2 < TT:
                    pool.wait_ge(o_add0, t + 1)
                    pool.wait_ge(o_add1, t + 1)
                    pool.dma_start(xres[:, t % 2, :], x_d[(t + 2) * P:(t + 3) * P, :]).then_inc(xres_in[t % 2], 16)

        @block.scalar
        def _(act):
            def split_hi(n):
                s = slices[n]
                act.wait_ge(raw_in[n % NRAW], raw_total[n])
                if NR <= n < S_UQ:
                    blk, k = (n - NR) // KD, n % KD
                    if k == KD - 1:
                        act.wait_ge(blk_done, (blk + 1) * TT)
                    else:
                        act.wait_ge(w_used, blk * (KD - 1) + k + 1)
                if S_AB + NR <= n < S_WO:
                    act.wait_ge(ab_done, ((n - S_AB - NR) // KU + 1) * TT)
                src = raw[:, n % NRAW, 0:s["n"]]
                if s["g"] is None:
                    act.activation(s["hi"], src, ACT.Copy).then_inc(hi_done, 1)
                else:
                    act.activation(s["hi"], src, ACT.Copy, scale=s["g"]).then_inc(hi_done, 1)

            def bank_ready(n):
                act.wait_ge(blk_done, n + 1)

            steps = [0]

            def link(ins):
                steps[0] += 1
                ins.then_inc(act_step, 1)
                act.wait_ge(act_step, steps[0])

            def rms(col, width):
                return act.activation(col, col, ACT.Sqrt, bias=eps[:, :], scale=1.0 / width)

            def square_x(t):
                act.wait_ge(x_in[t], 16)
                link(act.activation(junk_x[:, :], x_sb[t][:, :], ACT.Square, accum_out=ss[:, t:t + 1]))
                rms(ss[:, t:t + 1], DM).then_inc(x_sq, 1)

            def hT_hi(t):
                for c in range(2):
                    act.wait_ge(x_T, 2 * t + c + 1)
                    act.activation(hT_h[:, 4 * c:4 * c + 4, t * P:(t + 1) * P],
                                   ps[:, (2 * t + c) % 4, :].rearrange("p (k s) -> p k s", k=4), ACT.Copy).then_inc(hh_done, 1)

            def kz_copy(half):
                act.wait_ge(ka_T, half + 1)
                act.wait_ge(kz_zero, 2)
                cs = slice(half * W, (half + 1) * W)
                for g in range(AKV):
                    rs = slice(64 * g, 64 * g + 64)
                    act.activation(kz[rs, g, cs], ps[rs, 7, :], ACT.Copy).then_inc(kz_out, 1)

            def kvc(t):
                bank_ready(t)
                b = 4 + t % 3
                act.activation(ka[:, t, :], ps[:, b, 0:128], ACT.Copy)
                act.activation(va[:, t, :], ps[:, b, 128:256], ACT.Copy)
                act.activation(va_s[CHUNK:P, t, :], ps[0:CHUNK, b, 128:256], ACT.Copy)
                if t + 1 < TT:
                    act.activation(va_s[0:CHUNK, t + 1, :], ps[CHUNK:P, b, 128:256], ACT.Copy)
                act.activation(ckv[:, t, :], ps[:, b, 256:512], ACT.Copy).then_inc(kvc_out, 1)

            act.wait_ge(eps_set, 1)
            square_x(0)
            square_x(1)
            act.wait_ge(consts_in, 64)
            for n in range(4):
                split_hi(n)
            hT_hi(0)
            for n in range(4, 8):
                split_hi(n)
            for t in range(TT):
                if t + 2 < TT:
                    square_x(t + 2)
                if t + 1 < TT:
                    hT_hi(t + 1)
                if t == TT - 1:
                    for n in range(NR, NR + NRAW):
                        split_hi(n)
                kvc(t)
                if t == 4:
                    kz_copy(0)
            kz_copy(1)
            for n in range(NR + NRAW, 2 * NR):
                split_hi(n)
            for n in range(2 * NR, 3 * NR - 1):
                split_hi(n)
            for b in range(0, 8, 2):
                bank_ready(NB0 + b)
                act.activation(qaT[:, (b % 2) * 8:(b % 2 + 1) * 8, b // 2, :], ps[:, b, :].rearrange("p (c q) -> p c q", q=CHUNK),
                               ACT.Copy, scale=AD ** -0.5).then_inc(qa_out[0], 1)
            split_hi(3 * NR - 1)
            for n in range(3 * NR, 4 * NR - 1):
                split_hi(n)
            for t in range(TT):
                bank_ready(2 * TT + t)
                act.activation(ga[:, t, :], ps[:, t, :], ACT.Sigmoid).then_inc(ga_sig, 1)
            split_hi(4 * NR - 1)

            for n in range(A_STEPS + 1):
                m = n - LAG
                if 0 <= m < NCH:
                    act.wait_ge(a_T, m + 1)
                    if m >= NPA:
                        act.wait_ge(a_pv, m - NPA + 1)
                    act.activation(pT_a[:, m % NPA, :], ps[:, A_TB + m % 2, :], ACT.Copy).then_inc(a_pT, 1)
                if n < NCH:
                    lo = 0 if n else CHUNK
                    sm = small_a[:, n % NSM, :, :]
                    act.wait_ge(a_nmax, n + 1)
                    for e in range(AH // 2):
                        act.activation(s_a[:, n % NSA, e, lo:], s_a[:, n % NSA, e, lo:], ACT.Exp,
                                       bias=sm[:, 0, e:e + 1], accum_out=sm[:, 1, e:e + 1])
                    act.activation(sm[:, 3, :], sm[:, 2, :], ACT.Exp).then_inc(a_exp, 1)
                for t, k in filler(n - 1):
                    if t == TT - 1 and k < KD - 1:
                        split_hi(4 * NR + k)
                    if k == KD - 1:
                        bank_ready(3 * TT + t)
                        act.activation(cq[:, t, :], ps[:, t % 2, 0:QL], ACT.Copy)
                        act.activation(kr[:, t, :], ps[:, t % 2, QL:QL + BR], ACT.Copy).then_inc(cq_out, 1)
            split_hi(5 * NR - 1)
            act.wait_ge(cq_out, TT)
            act.wait_ge(a_out, TT)
            for t in range(TT):
                link(act.activation(junk_c[:, :], cq[:, t, :], ACT.Square, accum_out=ss[:, t:t + 1]))
                link(act.activation(junk_c[:, 0:KL], ckv[:, t, :], ACT.Square, accum_out=rstd[:, t:t + 1]))
            rms(ss, QL).then_inc(c_sq, 1)
            rms(rstd, KL).then_inc(c_sq, 1)
            for n in range(5 * NR, 6 * NR - 1):
                split_hi(n)
            for t in range(TT):
                bank_ready(4 * TT + t)
                act.activation(gb[:, t, :], ps[:, t, :], ACT.Sigmoid).then_inc(gb_sig, 1)
            split_hi(6 * NR - 1)
            for b in range(4):
                ahead = list(range((6 + b) * NR, (7 + b) * NR)) if b < 3 else list(range(S_UQ, S_UV))
                for n in ahead[:NR - 1]:
                    split_hi(n)
                for t in range(TT):
                    n = b * TT + t
                    bank_ready((5 + b) * TT + t)
                    if n >= NST:
                        act.wait_ge(gm_stored[n % NST], 16 * (n // NST))
                    act.activation(stage[:, n % NST, :], ps[:, t, :], ACT.Sigmoid).then_inc(gm_out, 1)
                for n in ahead[NR - 1:]:
                    split_hi(n)
            act.wait_ge(blk_done, NB)

            def q_copy(i, b0):
                act.activation(q_sb[:, i % 2, :], ps[:, b0:b0 + 2, :].rearrange("p b c -> p (b c)")[:, 0:BH * BQK],
                               ACT.Copy, scale=BQK ** -0.5).then_inc(q_out, 1)

            def qT_hi_out(i, b0):
                for c in range(2):
                    act.activation(qT_h[0:BQK, i % 2, 4 * c:4 * c + 4, :].rearrange("p h s -> p (h s)"),
                                   ps[0:BQK, b0 + c, :], ACT.Copy).then_inc(qT_hi, 1)

            for n, (kind, a, hf) in enumerate(KUSES):
                b = K_BANK + n % NKB
                cs = slice(hf * W, (hf + 1) * W)
                if n == 2:
                    for k in range(KK):
                        split_hi(S_UV + k)
                if n == N_CQ:
                    act.wait_ge(k_done, N_CQ)
                    for k in range(KK):
                        split_hi(S_UV + KK + k)
                if n == N_Q:
                    act.wait_ge(b_scores, 1)
                    q_copy(0, 0)
                if n == N_QT:
                    act.wait_ge(b_scores, 2)
                    qT_hi_out(0, 0)
                act.wait_ge(k_done, n + 1)
                if kind == "kr":
                    act.activation(kT_h[BN:BQK, 0, cs], ps[0:BR, b, :], ACT.Copy).then_inc(k_hi, 1)
                elif kind == "ckv":
                    act.activation(ckvT_h[:, hf, a, :], ps[:, b, :], ACT.Copy).then_inc(k_hi, 1)
                elif kind == "cq":
                    act.activation(cqT_h[:, a, cs], ps[:, b, :], ACT.Copy).then_inc(k_hi, 1)
                elif kind == "kn":
                    act.activation(kT_h[0:BN, 2 * a, cs], ps[0:BN, b, :], ACT.Copy)
                    act.activation(kT_h[0:BN, 2 * a + 1, cs], ps[BN:2 * BN, b, :], ACT.Copy).then_inc(k_hi, 1)
                elif a % 2:
                    if a < NST:
                        act.wait_ge(gm_stored[a], 16 * (4 * TT // NST))
                    act.activation(v_b[:, a, :], ps[:, b, :], ACT.Copy).then_inc(k_free[n % NKB], 1)

            for n in range(2, NU + LAG):
                if n >= LAG and USES[n - LAG][0] == "S":
                    for m, t0, t1 in PIECES[USES[n - LAG][1:]]:
                        if m % 2:
                            act.wait_ge(b_T, m + 1)
                            if m >= NPT:
                                act.wait_ge(b_pv, m - NPT + 1)
                            act.activation(pT_b[:, m % NPT, 0:(t1 - t0) * P], ps[:, 5, 0:(t1 - t0) * P], ACT.Copy)\
                                .then_inc(b_pT1, 1)
                if n < NU:
                    kind, i, h = USES[n]
                    b0 = SB[n]
                    if kind == "S":
                        m = SIDX[(i, h)]
                        keys = (i + 1) * P
                        act.wait_ge(b_nmax, m + 1)
                        if m >= NPB:
                            act.wait_ge(b_T, PIECES[(  (m - NPB) // BH, (m - NPB) % BH)][-1][0] + 1)
                        if h == 0 and i >= 2:
                            act.wait_ge(b_out, i - 1)
                        act.activation(p_b[:, m % NPB, 0:keys], span(b0, keys),
                                       ACT.Exp, bias=negm_b[:, m % 4:m % 4 + 1], accum_out=rs_b[:, i % 2, h:h + 1])\
                            .then_inc(b_exp, 1)
                        if i == TT - 1 and h < NR - 1:
                            split_hi(S_AB + h)
                    elif kind == "QT":
                        act.wait_ge(b_scores, n + 1)
                        qT_hi_out(i, b0)
                for j, late in ((n, False), (n - 1, True)):
                    if queries_of(j, late) is not None:
                        act.wait_ge(b_scores, j + 1)
                        q_copy(USES[j][1], SB[j])

            def u_hi_out(m):
                br, t = m // TT, m % TT
                act.wait_ge(u_T, m + 1)
                act.activation(uT_h[br][:, :, t * P:(t + 1) * P], ps[:, 6 + m % 2, :].rearrange("p (k s) -> p k s", k=KU),
                               ACT.Copy).then_inc(u_hi, 1)

            def m_hi_out(t):
                for c in range(2):
                    act.wait_ge(m_T, 2 * t + c + 1)
                    if t >= NMT:
                        act.wait_ge(o_done, 2 * (t - NMT + 1))
                    act.activation(mT_h[:, t % NMT, 4 * c:4 * c + 4, :].rearrange("p k s -> p (k s)"), ps[:, 6 + c, :],
                                   ACT.Copy).then_inc(m_hi, 1)

            u_hi_out(0)
            u_hi_out(1)
            for n in range(4 * TT):
                if n + 2 < 2 * TT:
                    u_hi_out(n + 2)
                if n == 1:
                    act.wait_ge(b_out, TT)
                    split_hi(S_AB + NR - 1)
                if n == TT:
                    for j in range(KU):
                        split_hi(S_AB + 2 * KU + j)
                if n == 2 * TT:
                    for j in range(KU):
                        split_hi(S_AB + 3 * KU + j)
                if n >= 2 * TT:
                    split_hi(S_WO + n - 2 * TT)
                if n in M_EARLY:
                    m_hi_out(M_EARLY.index(n))
            for t in range(TT):
                if t + 2 < TT:
                    m_hi_out(t + 2)
                act.wait_ge(o_done, 2 * t + 1)
                half0, half1 = ss[:, t:t + 1], rstd[:, t:t + 1]
                link(act.activation(junk_y[:, 0:W], ps[:, 2 * (t % 3), :], ACT.Square, accum_out=half0))
                link(act.activation(half0, half0, ACT.Identity, bias=eps[:, :], scale=1.0 / DM))
                act.wait_ge(o_done, 2 * t + 2)
                link(act.activation(junk_y[:, 0:W], ps[:, 2 * (t % 3) + 1, :], ACT.Square, accum_out=half1))
                act.activation(half1, half1, ACT.Sqrt, bias=half0, scale=1.0 / DM).then_inc(o_sq, 1)

        @block.vector
        def _(dve):
            steps = [0]

            def link(ins):
                steps[0] += 1
                ins.then_inc(dve_step, 1)
                dve.wait_ge(dve_step, steps[0])

            def invert(col):
                link(dve.reciprocal(col, col))

            def split_lo(n):
                s = slices[n]
                dve.wait_ge(hi_done, n + 1)
                src, hi = raw[:, n % NRAW, 0:s["n"]], s["hi"].bitcast(f32)
                if s["g"] is None:
                    dve.tensor_tensor(s["lo"], src, hi, ALU.subtract).then_inc(lo_done, 1)
                else:
                    dve.scalar_tensor_tensor(s["lo"], src, s["g"], hi, ALU.mult, ALU.subtract).then_inc(lo_done, 1)

            def norm_x(t):
                dve.wait_ge(x_sq, t + 1)
                invert(ss[:, t:t + 1])
                dve.tensor_scalar(x_sb[t][:, :], x_sb[t][:, :], ss[:, t:t + 1], None, ALU.mult).then_inc(x_norm, 1)

            def hT_lo(t):
                for c in range(2):
                    dve.wait_ge(hh_done, 2 * t + c + 1)
                    ks, cs = slice(4 * c, 4 * c + 4), slice(t * P, (t + 1) * P)
                    dve.tensor_tensor(hT_l[:, ks, cs], ps[:, (2 * t + c) % 4, :].rearrange("p (k s) -> p k s", k=4),
                                      hT_h[:, ks, cs].bitcast(f32), ALU.subtract).then_inc(hl_done, 1)

            dve.memset(eps[:, :], EPS).then_inc(eps_set, 1)
            norm_x(0)
            norm_x(1)
            for n in range(4):
                split_lo(n)
            hT_lo(0)
            for n in range(4, 8):
                split_lo(n)
            for t in range(TT):
                if t + 2 < TT:
                    norm_x(t + 2)
                if t + 1 < TT:
                    hT_lo(t + 1)
            for n in range(NR, NR + NRAW):
                split_lo(n)
            for n in range(NR + NRAW, 3 * NR - 1):
                split_lo(n)
            for b in range(1, 8, 2):
                dve.wait_ge(blk_done, NB0 + b + 1)
                dve.tensor_scalar(qaT[:, (b % 2) * 8:(b % 2 + 1) * 8, b // 2, :], ps[:, b, :].rearrange("p (c q) -> p c q", q=CHUNK),
                                  AD ** -0.5, None, ALU.mult).then_inc(qa_out[1], 1)
            for n in range(3 * NR - 1, 4 * NR - 1):
                split_lo(n)
            for t in range(TT):
                dve.wait_ge(ga_sig, t + 1)
                dve.tensor_tensor(ga[:, t, :], ps[:, t, :], ga[:, t, :], ALU.mult).then_inc(ga_done, 1)
            split_lo(4 * NR - 1)

            def mark(ins):
                steps[0] += 1
                ins.then_inc(dve_step, 1)
                return steps[0]

            def need(done):
                dve.wait_ge(dve_step, done)

            dve.wait_ge(late_in, 48)
            link(dve.tensor_scalar(nsink, sink, -1.0, None, ALU.mult))
            dve.wait_ge(first_zero, 2)
            for n in range(NCH + LAG_N):
                soft, norm = n < NCH, n >= LAG_N
                if soft:
                    lo = 0 if n else CHUNK
                    negm, esink = small_a[:, n % NSM, 0, :], small_a[:, n % NSM, 2, :]
                    s_n = s_a[:, n % NSA, :, lo:]
                    dve.wait_ge(a_scores, n + 1)
                    if n >= NSA:
                        dve.wait_ge(a_T, n - NSA + 1)
                    dve.tensor_tensor(s_n, ps[:, A_SB + n % 2, :].rearrange("p (e c) -> p e c", c=P)[:, :, lo:],
                                      alibi[:, :, lo:], ALU.add).then_inc(a_added, 1)
                if norm:
                    k = n - LAG_N
                    i, e = k // 2, k % 2
                    den = small_a[:, k % NSM, 4, :]
                    dve.wait_ge(a_pv, k + 1)
                    den_set = mark(dve.tensor_tensor(den, small_a[:, k % NSM, 1, :], small_a[:, k % NSM, 3, :], ALU.add))
                if soft:
                    dve.wait_ge(a_added, n + 1)
                    max_set = mark(dve.tensor_reduce(negm, s_n, AX.X, ALU.max, negate=True))
                if norm:
                    need(den_set)
                    inv_set = mark(dve.reciprocal(den, den))
                if soft:
                    need(max_set)
                    min_set = mark(dve.tensor_tensor(negm, negm, nsink, ALU.min))

                def norm_half(j):
                    rs = slice(CHUNK * j, CHUNK * (j + 1))
                    out = onorm_a[CHUNK * e:CHUNK * (e + 1), i % 2, :].rearrange("p (u j d) -> p u j d", j=2, d=AD)[:, :, j, :]
                    return dve.tensor_tensor(out, ps[rs, A_OB + k % 2, 0:4 * AD].rearrange("p (u d) -> p u d", d=AD),
                                             den[rs, :].unsqueeze(2).to_broadcast([CHUNK, AH // 2, AD]), ALU.mult)

                if norm:
                    need(inv_set)
                    if i >= 2:
                        dve.wait_ge(a_out, i - 1)
                    norm_half(0)
                if soft:
                    need(min_set)
                    dve.tensor_tensor(esink, negm, sink, ALU.add).then_inc(a_nmax, 1)
                if norm:
                    norm_half(1).then_inc(a_norm, 1)
                for t, j in filler(n - 1):
                    if t == TT - 1 and j < KD - 1:
                        split_lo(4 * NR + j)

            split_lo(5 * NR - 1)
            dve.wait_ge(c_sq, 2)
            invert(ss)
            invert(rstd)
            for t in range(TT):
                dve.tensor_scalar(cq[:, t, :], cq[:, t, :], ss[:, t:t + 1], None, ALU.mult).then_inc(c_norm, 1)
                dve.tensor_scalar(ckv[:, t, :], ckv[:, t, :], rstd[:, t:t + 1], None, ALU.mult).then_inc(c_norm, 1)
            dve.wait_ge(rope_in, 16)
            H2 = BR // 2
            cosr, sinr = rope[:, 0, :, :], rope[:, 1, :, :]
            dve.tensor_tensor(krr[:, :, 0:H2], kr[:, :, 0:H2], cosr, ALU.mult)
            dve.tensor_tensor(krr[:, :, H2:], kr[:, :, H2:], cosr, ALU.mult)
            dve.tensor_tensor(kr2[:, :, 0:H2], kr[:, :, H2:], sinr, ALU.mult)
            link(dve.tensor_tensor(kr2[:, :, H2:], kr[:, :, 0:H2], sinr, ALU.mult))
            dve.tensor_tensor(krr[:, :, 0:H2], krr[:, :, 0:H2], kr2[:, :, 0:H2], ALU.subtract)
            dve.tensor_tensor(krr[:, :, H2:], krr[:, :, H2:], kr2[:, :, H2:], ALU.add).then_inc(kr_roped, 1)

            for n in range(5 * NR, 6 * NR - 1):
                split_lo(n)
            for t in range(TT):
                dve.wait_ge(gb_sig, t + 1)
                dve.tensor_tensor(gb[:, t, :], ps[:, t, :], gb[:, t, :], ALU.mult).then_inc(gb_done, 1)
            for n in range(6 * NR - 1, S_UV):
                split_lo(n)

            def rope_q(i):
                r = q_sb[:, i % 2, :].rearrange("p (h c) -> p h c", h=BH)
                x1, x2 = r[:, :, BN:BN + H2], r[:, :, BN + H2:]
                cb_, sb_ = (rope_b[:, e, i, :].unsqueeze(1).to_broadcast([P, BH, H2]) for e in range(2))
                tmp = onorm_b[:, :].rearrange("p (e h c) -> p e h c", e=4, h=BH)
                dve.tensor_tensor(tmp[:, 0], x1, sb_, ALU.mult)
                dve.tensor_tensor(tmp[:, 1], x2, sb_, ALU.mult)
                dve.tensor_tensor(tmp[:, 2], x1, cb_, ALU.mult)
                link(dve.tensor_tensor(tmp[:, 3], x2, cb_, ALU.mult))
                dve.tensor_tensor(x1, tmp[:, 2], tmp[:, 1], ALU.subtract)
                dve.tensor_tensor(x2, tmp[:, 3], tmp[:, 0], ALU.add).then_inc(q_roped, 1)

            def qT_lo_out(i, b0):
                for c in range(2):
                    dve.wait_ge(qT_hi, 2 * i + c + 1)
                    hs = slice(4 * c, 4 * c + 4)
                    dve.tensor_tensor(qT_l[0:BQK, i % 2, hs, :].rearrange("p h s -> p (h s)"), ps[0:BQK, b0 + c, :],
                                      qT_h[0:BQK, i % 2, hs, :].rearrange("p h s -> p (h s)").bitcast(f32),
                                      ALU.subtract).then_inc(qT_lo, 1)

            for n, (kind, a, hf) in enumerate(KUSES):
                b = K_BANK + n % NKB
                cs = slice(hf * W, (hf + 1) * W)
                if n == 2:
                    for k in range(KK):
                        split_lo(S_UV + k)
                if n == N_CQ:
                    for k in range(KK):
                        split_lo(S_UV + KK + k)
                if n == N_Q + 1:
                    dve.wait_ge(q_out, 1)
                    dve.wait_ge(rope_in, 32)
                    rope_q(0)
                if n == N_QT:
                    qT_lo_out(0, 0)
                if kind == "v":
                    if a % 2 == 0:
                        dve.wait_ge(k_done, n + 1)
                        if a < NST:
                            dve.wait_ge(gm_stored[a], 16 * (4 * TT // NST))
                        dve.tensor_copy(v_b[:, a, :], ps[:, b, :]).then_inc(k_free[n % NKB], 1)
                    continue
                dve.wait_ge(k_hi, K_SPLIT.index(n) + 1)
                if kind == "kr":
                    ins = dve.tensor_tensor(kT_l[BN:BQK, 0, cs], ps[0:BR, b, :], kT_h[BN:BQK, 0, cs].bitcast(f32), ALU.subtract)
                elif kind == "ckv":
                    ins = dve.tensor_tensor(ckvT_l[:, hf, a, :], ps[:, b, :], ckvT_h[:, hf, a, :].bitcast(f32), ALU.subtract)
                elif kind == "cq":
                    ins = dve.tensor_tensor(cqT_l[:, a, cs], ps[:, b, :], cqT_h[:, a, cs].bitcast(f32), ALU.subtract)
                else:
                    dve.tensor_tensor(kT_l[0:BN, 2 * a, cs], ps[0:BN, b, :], kT_h[0:BN, 2 * a, cs].bitcast(f32), ALU.subtract)
                    ins = dve.tensor_tensor(kT_l[0:BN, 2 * a + 1, cs], ps[BN:2 * BN, b, :],
                                            kT_h[0:BN, 2 * a + 1, cs].bitcast(f32), ALU.subtract)
                ins.then_inc(k_free[n % NKB], 1)

            for n in range(2, NU + LAG_N):
                if LAG <= n < NU + LAG and USES[n - LAG][0] == "S":
                    for m, t0, t1 in PIECES[USES[n - LAG][1:]]:
                        if m % 2 == 0:
                            dve.wait_ge(b_T, m + 1)
                            if m >= NPT:
                                dve.wait_ge(b_pv, m - NPT + 1)
                            dve.tensor_copy(pT_b[:, m % NPT, 0:(t1 - t0) * P], ps[:, 4, 0:(t1 - t0) * P]).then_inc(b_pT0, 1)
                if 2 < n <= NU and USES[n - 1][0] == "QT":
                    qT_lo_out(USES[n - 1][1], SB[n - 1])
                if n < NU:
                    kind, i, h = USES[n]
                    b0 = SB[n]
                    if kind == "S":
                        m = SIDX[(i, h)]
                        dve.wait_ge(b_scores, n + 1)
                        if m >= 4:
                            dve.wait_ge(b_exp, m - 3)
                        dve.tensor_reduce(negm_b[:, m % 4:m % 4 + 1],
                                          span(b0, (i + 1) * P),
                                          AX.X, ALU.max, negate=True).then_inc(b_nmax, 1)
                        if i == TT - 1 and h > 0:
                            split_lo(S_AB + h - 1)
                if 1 < n - ROPE_LAG < NU and USES[n - ROPE_LAG][0] == "Q":
                    i = USES[n - ROPE_LAG][1]
                    dve.wait_ge(q_out, i + 1)
                    if i >= 2:
                        dve.wait_ge(b_out, i - 1)
                    rope_q(i)
                if n >= LAG_N and USES[n - LAG_N][0] == "S" and USES[n - LAG_N][2] == BH - 1:
                    i = USES[n - LAG_N][1]
                    dve.wait_ge(b_pv, PIECES[(i, BH - 1)][-1][0] + 1)
                    dve.wait_ge(q_roped, min(TT, i + 2))
                    link(dve.reciprocal(rden_b[:, :], rs_b[:, i % 2, :]))
                    o8 = onorm_b[:, :].rearrange("p (h d) -> p h d", h=BH)
                    link(dve.tensor_tensor(o8, ps[:, 6 + i % 2, :].rearrange("p (h d) -> p h d", h=BH),
                                           rden_b[:, :].unsqueeze(2).to_broadcast([P, BH, BV]), ALU.mult))
                    dve.tensor_tensor(gb[:, i, :], onorm_b[:, :], gb[:, i, :], ALU.mult).then_inc(b_out, 1)

            def u_lo_out(m):
                br, t = m // TT, m % TT
                dve.wait_ge(u_hi, m + 1)
                cs = slice(t * P, (t + 1) * P)
                dve.tensor_tensor(uT_l[br][:, :, cs], ps[:, 6 + m % 2, :].rearrange("p (k s) -> p k s", k=KU),
                                  uT_h[br][:, :, cs].bitcast(f32), ALU.subtract).then_inc(u_lo, 1)

            def m_lo_out(t):
                for c in range(2):
                    dve.wait_ge(m_hi, 2 * t + c + 1)
                    ks = slice(4 * c, 4 * c + 4)
                    dve.tensor_tensor(mT_l[:, t % NMT, ks, :].rearrange("p k s -> p (k s)"), ps[:, 6 + c, :],
                                      mT_h[:, t % NMT, ks, :].rearrange("p k s -> p (k s)").bitcast(f32),
                                      ALU.subtract).then_inc(m_lo, 1)

            u_lo_out(0)
            u_lo_out(1)
            for n in range(4 * TT):
                if n + 2 < 2 * TT:
                    u_lo_out(n + 2)
                cb, t = (n // TT) % 2, n % TT
                dve.wait_ge(gate_in[n % NG], 16 * (n // NG + 1))
                dve.wait_ge(ab_done, n + 1)
                dst = merged[:, t, cb * W:(cb + 1) * W] if n < 2 * TT else gate[:, n % NG, :]
                dve.tensor_tensor(dst, ps[:, n % 6, :], gate[:, n % NG, :], ALU.mult).then_inc(ab_out, 1)
                if n == 1:
                    split_lo(S_AB + NR - 1)
                if n == TT:
                    for j in range(KU):
                        split_lo(S_AB + 2 * KU + j)
                if n == 2 * TT:
                    for j in range(KU):
                        split_lo(S_AB + 3 * KU + j)
                if n >= 2 * TT:
                    split_lo(S_WO + n - 2 * TT)
                if n in M_EARLY:
                    m_lo_out(M_EARLY.index(n))
            dve.wait_ge(late_in, 64)
            for t in range(TT):
                if t + 2 < TT:
                    m_lo_out(t + 2)
                dve.wait_ge(o_sq, t + 1)
                invert(rstd[:, t:t + 1])
                if t >= 2:
                    dve.wait_ge(stored[t % 2], 2 * 16 * (t // 2))
                y = y_sb[:, t % 2, :]
                for c in range(2):
                    cs = slice(c * W, (c + 1) * W)
                    dve.scalar_tensor_tensor(y[:, cs], ps[:, 2 * (t % 3) + c, :], rstd[:, t:t + 1], pg[:, cs],
                                             ALU.mult, ALU.mult).then_inc(o_y, 1)
                dve.wait_ge(o_y, 2 * t + 2)
                dve.wait_ge(xres_in[t % 2], 16 * (t // 2 + 1))
                dve.tensor_tensor(y[:, W:], y[:, W:], xres[:, t % 2, W:], ALU.add).then_inc(o_add1, 1)

        @block.tensor
        def _(pe):
            mm = nc.tensor.matmul

            def product(out, l_h, l_l, r_h, r_l, first, last):
                mm(out, l_h, r_h, start=first, stop=False)
                mm(out, l_h, r_l, start=False, stop=False)
                return mm(out, l_l, r_h, start=False, stop=last)

            def turn(out, src):
                return nc.tensor.transpose(out, src, ident[0:src.shape[0], 0:src.shape[0]])

            def x_turn(t):
                pe.wait_ge(x_norm, t + 1)
                for c in range(2):
                    b = (2 * t + c) % 4
                    if t >= 2:
                        pe.wait_ge(hl_done, 2 * (t - 2) + c + 1)
                    for k in range(4):
                        ins = turn(ps[:, b, k * P:(k + 1) * P], x_sb[t][:, (4 * c + k) * P:(4 * c + k + 1) * P])
                    ins.then_inc(x_T, 1)

            def ka_turn(t):
                pe.wait_ge(kvc_out, t + 1)
                if t == 4:
                    pe.wait_ge(kz_out, 2)
                ins = turn(ps[:, 7, (t % 4) * P:(t % 4 + 1) * P], ka[:, t, :])
                if t % 4 == 3:
                    ins.then_inc(ka_T, 1)

            def tokens_tile(t, k, blk, n, bank):
                s, cs = (blk * NR + k) % NR, slice(t * P, (t + 1) * P)
                return product(ps[:, bank, 0:n], hT_h[:, k, cs], hT_l[:, k, cs], w_h[:, s, 0:n], w_l[:, s, 0:n],
                               k == 0, k == KD - 1)

            pe.wait_ge(consts_in, 64)
            x_turn(0)
            for t in range(TT):
                if t + 1 < TT:
                    x_turn(t + 1)
                pe.wait_ge(hl_done, 2 * t + 2)
                if t >= 3:
                    pe.wait_ge(kvc_out, t - 2)
                for k in range(KD):
                    if t == 0:
                        pe.wait_ge(lo_done, k + 1)
                    ins = tokens_tile(t, k, 0, W, 4 + t % 3)
                    if k == KD - 1:
                        ins.then_inc(blk_done, 1)
                    elif t == TT - 1:
                        ins.then_inc(w_used, 1)
                if t >= 1:
                    ka_turn(t - 1)
            ka_turn(TT - 1)

            pe.wait_ge(hl_done, 2 * TT)
            for k in range(KD):
                s = NR + k
                pe.wait_ge(lo_done, s + 1)
                for b in range(8):
                    j, cs = b // 2, slice((b % 2) * W, (b % 2 + 1) * W)
                    if k == 0 and 4 <= b <= 6:
                        pe.wait_ge(kvc_out, TT)
                    if k == 0 and b == 7:
                        pe.wait_ge(kz_out, 4)
                    ls = slice(j * P, (j + 1) * P)
                    ins = product(ps[:, b, :], w_h[:, k, ls], w_l[:, k, ls], hT_h[:, k, cs], hT_l[:, k, cs],
                                  k == 0, k == KD - 1)
                    if k == KD - 1:
                        ins.then_inc(blk_done, 1)
                if k < KD - 1:
                    ins.then_inc(w_used, 1)

            def tokens_block(blk, n, bank_free):
                for k in range(KD):
                    pe.wait_ge(lo_done, blk * NR + k + 1)
                    for t in range(TT):
                        if k == 0:
                            bank_free(t)
                        ins = tokens_tile(t, k, blk, n, t)
                        if k == KD - 1:
                            ins.then_inc(blk_done, 1)
                    if k < KD - 1:
                        ins.then_inc(w_used, 1)

            tokens_block(2, W, lambda t: pe.wait_ge(qa_out[t % 2], t // 2 + 1))

            for n in range(A_STEPS):
                m = n - LAG
                if 0 <= m < NCH:
                    pe.wait_ge(a_exp, m + 1)
                    if m < 2:
                        pe.wait_ge(ga_done, A_TB + m + 1)
                    else:
                        pe.wait_ge(a_pT, m - 1)
                    for e in range(AH // 2):
                        ins = turn(ps[:, A_TB + m % 2, e * P:(e + 1) * P], s_a[:, m % NSA, e, :])
                    ins.then_inc(a_T, 1)
                for t, k in filler(n):
                    if k == 0:
                        pe.wait_ge(*((ga_done, t + 1) if t < 2 else (cq_out, t - 1)))
                    if t == 0:
                        pe.wait_ge(lo_done, 3 * NR + k + 1)
                    ins = tokens_tile(t, k, 3, QL + BR, t % 2)
                    if k == KD - 1:
                        ins.then_inc(blk_done, 1)
                    elif t == TT - 1:
                        ins.then_inc(w_used, 1)
                if n < NCH:
                    if n < 2:
                        pe.wait_ge(ga_done, A_SB + n + 1)
                    else:
                        pe.wait_ge(a_added, n - 1)
                    lo = 0 if n else CHUNK
                    ks = slice((n - 1) * CHUNK + lo, (n + 1) * CHUNK)
                    for g in range(AKV):
                        for p in range(2):
                            js, c0 = slice(2 * p, 2 * p + 2), (2 * g + p) * P
                            ins = mm(ps[:, A_SB + n % 2, c0 + lo:c0 + P], qaT[:, n, js, :].rearrange("p j q -> p (j q)"),
                                     kz[:, g, ks], start=True, stop=True)
                    ins.then_inc(a_scores, 1)
                m = n - LAG_V
                if m >= 0:
                    if m < 2:
                        pe.wait_ge(ga_done, A_OB + m + 1)
                    else:
                        pe.wait_ge(a_norm, m - 1)
                    pe.wait_ge(a_pT, m + 1)
                    vals = (va_s, va)[m % 2]
                    for e in range(AH // 2):
                        g = e // 2
                        ins = mm(ps[:, A_OB + m % 2, e * AD:(e + 1) * AD], pT_a[:, m % NPA, e * P:(e + 1) * P],
                                 vals[:, m // 2, g * AD:(g + 1) * AD], start=True, stop=True)
                    ins.then_inc(a_pv, 1)

            def after_a(t):
                pe.wait_ge(*((cq_out, TT - 1 + t) if t < A_SB else (a_added, NCH) if t < A_TB else
                             (a_pT, NCH) if t < A_OB else (a_norm, NCH)))

            tokens_block(4, W, after_a)
            for b in range(4):
                tokens_block(5 + b, W, lambda t: pe.wait_ge(gb_done, t + 1) if b == 0 else pe.wait_ge(gm_out, (b - 1) * TT + t + 1))

            pe.wait_ge(kr_roped, 1)
            pe.wait_ge(c_norm, 2 * TT)

            def q_tile(i, b0):
                ts = slice(i * P, (i + 1) * P)
                for c0, c1, b in ((0, W, b0), (W, BH * BQK, b0 + 1)):
                    for k in range(KQ):
                        ins = product(ps[:, b, 0:c1 - c0], cqT_h[:, k, ts], cqT_l[:, k, ts],
                                      wuq_h[:, k, c0:c1], wuq_l[:, k, c0:c1], k == 0, k == KQ - 1)
                return ins

            def q_turn(i, b0):
                pe.wait_ge(q_roped, i + 1)
                for h in range(BH):
                    ins = turn(ps[0:BQK, b0 + h // 4, (h % 4) * P:(h % 4 + 1) * P], q_sb[:, i % 2, h * BQK:(h + 1) * BQK])
                return ins

            def k_read_out(b):
                if b >= K_BANK:
                    pe.wait_ge(k_free[b - K_BANK], K_LAST[b - K_BANK])

            for n, (kind, a, hf) in enumerate(KUSES):
                b = K_BANK + n % NKB
                if n == N_Q:
                    for m in range(N_Q):
                        if KUSES[m][0] == "cq" and KUSES[m][2] == 0:
                            pe.wait_ge(k_free[m % NKB], m // NKB + 1)
                    pe.wait_ge(gm_out, 3 * TT + 2)
                    q_tile(0, 0).then_inc(b_scores, 1)
                if n == N_QT:
                    q_turn(0, 0).then_inc(b_scores, 1)
                if n < NKB:
                    pe.wait_ge(gm_out, 3 * TT + b + 1)
                else:
                    pe.wait_ge(k_free[n % NKB], n // NKB)
                cs = slice(hf * W, (hf + 1) * W)
                if kind in ("kr", "ckv", "cq"):
                    for j in range(4):
                        t = 4 * hf + j
                        src = {"kr": krr, "ckv": ckv, "cq": cq}[kind]
                        if kind == "kr":
                            ins = turn(ps[0:BR, b, j * P:(j + 1) * P], src[:, t, :])
                        else:
                            ins = turn(ps[:, b, j * P:(j + 1) * P], src[:, t, a * P:(a + 1) * P])
                elif kind == "v":
                    if a == 0:
                        pe.wait_ge(lo_done, S_UV + KK)
                    for c in range(KK):
                        m = KUSES.index(("ckv", c, a // 4))
                        pe.wait_ge(k_free[m % NKB], m // NKB + 1)
                    ts = slice((a % 4) * P, (a % 4 + 1) * P)
                    for k in range(KK):
                        ins = product(ps[:, b, :], ckvT_h[:, a // 4, k, ts], ckvT_l[:, a // 4, k, ts], wv_h[:, k, :], wv_l[:, k, :],
                                      k == 0, k == KK - 1)
                else:
                    if a == 0:
                        pe.wait_ge(lo_done, S_AB)
                    ls = slice(a * P, (a + 1) * P)
                    for k in range(KK):
                        ins = product(ps[:, b, :], wk_h[:, k, ls], wk_l[:, k, ls], ckvT_h[:, hf, k, :], ckvT_l[:, hf, k, :],
                                      k == 0, k == KK - 1)
                ins.then_inc(k_done, 1)

            for n in range(2, NU + LAG_V):
                if LAG <= n < NU + LAG and USES[n - LAG][0] == "S":
                    _, i, h = USES[n - LAG]
                    pe.wait_ge(b_exp, SIDX[(i, h)] + 1)
                    for m, t0, t1 in PIECES[(i, h)]:
                        if m >= 2:
                            pe.wait_ge((b_pT0, b_pT1)[m % 2], m // 2)
                        else:
                            k_read_out(4 + m)
                        for t in range(t0, t1):
                            ins = turn(ps[:, 4 + m % 2, (t - t0) * P:(t - t0 + 1) * P],
                                       p_b[:, SIDX[(i, h)] % NPB, t * P:(t + 1) * P])
                        ins.then_inc(b_T, 1)
                if n < NU:
                    kind, i, h = USES[n]
                    b0 = SB[n]
                    if not BEFORE[n]:
                        k_read_out(b0)
                    for before in BEFORE[n]:
                        pk, pi, ph = USES[before]
                        if pk == "S":
                            pe.wait_ge(b_exp, SIDX[(pi, ph)] + 1)
                        elif pk == "Q":
                            pe.wait_ge(q_out, pi + 1)
                        else:
                            pe.wait_ge(qT_lo, 2 * pi + 2)
                    if kind == "Q":
                        ins = q_tile(i, b0)
                    elif kind == "QT":
                        ins = q_turn(i, b0)
                    else:
                        if h == 0:
                            pe.wait_ge(qT_lo, 2 * i + 2)
                        if (i, h) == (0, 0):
                            pe.wait_ge(kr_spread, 3 * 16)
                            pe.wait_ge(mask_in, 16)
                            pe.wait_ge(mask_q, 2)
                        if (i, h) == (1, 0):
                            pe.wait_ge(mask_q, 5)
                        if i >= 2:
                            pe.wait_ge(mask_k, (i - 2) * BH + h + 1)
                        a = i % 2
                        for t0 in range(0, i + 1, 4):
                            t1 = min(i + 1, t0 + 4)
                            ks = slice(t0 * P, t1 * P)
                            out = ps[:, b0 + t0 // 4, 0:(t1 - t0) * P]
                            mm(out, qT_h[0:BQK + 2, a, h, :], kT_h[0:BQK + 2, h, ks], start=True, stop=False)
                            mm(out, qT_h[0:BQK, a, h, :], kT_l[0:BQK, h, ks], start=False, stop=False)
                            ins = mm(out, qT_l[0:BQK, a, h, :], kT_h[0:BQK, h, ks], start=False, stop=True)
                    ins.then_inc(b_scores, 1)
                if n >= LAG_V and USES[n - LAG_V][0] == "S":
                    _, i, h = USES[n - LAG_V]
                    if h == 0 and i < 2:
                        k_read_out(6 + i)
                    if h == 0 and i >= 2:
                        pe.wait_ge(b_out, i - 1)
                    for m, t0, t1 in PIECES[(i, h)]:
                        pe.wait_ge((b_pT0, b_pT1)[m % 2], m // 2 + 1)
                        for t in range(t0, t1):
                            ins = mm(ps[:, 6 + i % 2, h * BV:(h + 1) * BV], pT_b[:, m % NPT, (t - t0) * P:(t - t0 + 1) * P],
                                     v_b[:, t, h * BV:(h + 1) * BV], start=(t == 0), stop=(t == i))
                        ins.then_inc(b_pv, 1)

            def u_turn(m):
                br, t = m // TT, m % TT
                if m == 0:
                    pe.wait_ge(b_out, TT - 1)
                if m == 1:
                    pe.wait_ge(b_out, TT)
                if m >= 2:
                    pe.wait_ge(u_lo, m - 1)
                for k in range(KU):
                    ins = turn(ps[:, 6 + m % 2, k * P:(k + 1) * P], (ga, gb)[br][:, t, k * P:(k + 1) * P])
                ins.then_inc(u_T, 1)

            def m_turn(t):
                pe.wait_ge(g_add, TT + t + 1)
                for c in range(2):
                    if t == 0:
                        pe.wait_ge(u_lo, 2 * TT)
                    else:
                        pe.wait_ge(m_lo, 2 * (t - 1) + c + 1)
                    for k in range(4):
                        ins = turn(ps[:, 6 + c, k * P:(k + 1) * P], merged[:, t, (4 * c + k) * P:(4 * c + k + 1) * P])
                    ins.then_inc(m_T, 1)

            u_turn(0)
            u_turn(1)
            for n in range(4 * TT):
                if n + 2 < 2 * TT:
                    u_turn(n + 2)
                blk, t = n // TT, n % TT
                br, s0, cs = blk // 2, (blk % 2) * KU, slice(t * P, (t + 1) * P)
                if n == 0:
                    pe.wait_ge(b_exp, len(SIDX))
                    pe.wait_ge(b_pT0, (npiece + 1) // 2)
                    pe.wait_ge(b_pT1, npiece // 2)
                if n >= 6:
                    pe.wait_ge(ab_out, n - 5)
                pe.wait_ge(u_lo, br * TT + t + 1)
                if t == 0:
                    pe.wait_ge(lo_done, S_AB + (blk + 1) * KU)
                for k in range(KU):
                    ins = product(ps[:, n % 6, :], uT_h[br][:, k, cs], uT_l[br][:, k, cs],
                                  w_h[:, s0 + k, :], w_l[:, s0 + k, :], k == 0, k == KU - 1)
                ins.then_inc(ab_done, 1)
                if n in M_EARLY:
                    m_turn(M_EARLY.index(n))

            pe.wait_ge(ab_out, 4 * TT)
            pe.wait_ge(lo_done, NS)
            for t in range(TT):
                if t + 2 < TT:
                    m_turn(t + 2)
                if t >= 3:
                    pe.wait_ge(o_y, 2 * (t - 2))
                pe.wait_ge(m_lo, 2 * t + 2)
                for cb in range(2):
                    for k in range(KD):
                        ins = product(ps[:, 2 * (t % 3) + cb, :], mT_h[:, t % NMT, k, :], mT_l[:, t % NMT, k, :],
                                      wo_h[2 * k + cb][:, :], wo_l[2 * k + cb][:, :], k == 0, k == KD - 1)
                    ins.then_inc(o_done, 1)


_INS = ["x", "pre_norm_g", "w_in", "a_sinks", "b_q_norm_g", "b_w_uq", "b_kv_norm_g", "b_w_ukv",
        "a_w_o", "b_w_o", "w_out", "post_norm_g"]


def kernel(**inputs):
    import concourse.bacc as bacc
    from concourse.bass_utils import run_bass_kernel_spmd

    nc = bacc.Bacc("TRN2", target_bir_lowering=False, num_devices=1)
    arrays, args = {}, []
    feeds = [(n, np.ascontiguousarray(np.asarray(inputs[n])[0])) for n in _INS]
    feeds = [(n, np.ascontiguousarray(a.reshape(-1, P).T) if n in ("pre_norm_g", "b_q_norm_g", "b_kv_norm_g") else a)
             for n, a in feeds]
    feeds = [(n, np.ascontiguousarray(a.reshape(AH // 2, 2).T) if n == "a_sinks" else a) for n, a in feeds]
    feeds += [("ident", np.eye(P, dtype=np.float32)), ("rope", rope_table()), ("alibi", alibi_table()),
              ("mask", mask_rows())]
    for name, a in feeds:
        arrays[f"in_{name}"] = a
        args.append(nc.dram_tensor(f"in_{name}", a.shape, mybir.dt.from_np(a.dtype), kind="ExternalInput").ap())
    out = nc.dram_tensor("out", (SEQ, DM), mybir.dt.float32, kind="ExternalOutput").ap()
    build(nc, *args, out)
    r = run_bass_kernel_spmd(nc, [arrays], core_ids=[0])
    return r.results[0]["out"].reshape(1, SEQ, DM)
```
